# Optimizing a Trainium2 kernel written in Bass

```python
import jax
import jax.numpy as jnp
from jax import lax
import numpy as np

D_MODEL = 2048
BATCH = 1
SEQ = 256
DEPTH = 2

N_EVEN = (DEPTH + 1) // 2
N_ODD = DEPTH // 2

FOX_HEADS = 8
FOX_HEAD_DIM = 128
FOX_WIDTH = FOX_HEADS * FOX_HEAD_DIM
Q_BLOCK = 128

RWKV_HEAD_DIM = 64
RWKV_WIDTH = D_MODEL - FOX_WIDTH
RWKV_HEADS = RWKV_WIDTH // RWKV_HEAD_DIM
DECAY_RANK = 96
ICLR_RANK = 96
GATE_RANK = 256
GN_EPS = 64e-5

FOX_COLS = 3 * FOX_WIDTH + FOX_HEADS
RWKV_COLS = 3 * RWKV_WIDTH + DECAY_RANK + ICLR_RANK + GATE_RANK
IN_COLS = FOX_COLS + RWKV_COLS

POOL_WINDOWS = (2, 4, 8, 16)
POOL_GROUPS = len(POOL_WINDOWS)
POOL_GROUP_DIM = D_MODEL // POOL_GROUPS

D_FF = 5632
CONV_WIDTH = 3
RMS_EPS = 1e-6

kernel_name = 'fox_rwkv7_pool_hybrid'

def rmsnorm(x, g):
    xf = x.astype(jnp.float32)
    y = xf * lax.rsqrt(jnp.mean(xf * xf, axis=-1, keepdims=True) + RMS_EPS)
    return (y * g.astype(jnp.float32)).astype(x.dtype)

def token_shift(x):
    return jnp.pad(x, ((0, 0), (1, 0), (0, 0)))[:, :-1]

def forgetting_attention(q, k, v, log_f):
    B, S, H, Dh = q.shape
    nb = S // Q_BLOCK
    c = jnp.cumsum(log_f, axis=1)
    c_keys = c.transpose(0, 2, 1)
    q_blocks = q.reshape(B, nb, Q_BLOCK, H, Dh).transpose(1, 0, 3, 2, 4)
    c_blocks = c.reshape(B, nb, Q_BLOCK, H).transpose(1, 0, 3, 2)
    k_pos = jnp.arange(S)
    scale = Dh ** -0.5

    def one_block(args):
        i, q_i, c_i = args
        s = jnp.einsum('bhqd,bkhd->bhqk', q_i, k, preferred_element_type=jnp.float32) * scale
        s = s + (c_i[..., :, None] - c_keys[..., None, :])
        q_pos = i * Q_BLOCK + jnp.arange(Q_BLOCK)
        causal = k_pos[None, :] <= q_pos[:, None]
        s = jnp.where(causal, s, -jnp.inf)
        p = jax.nn.softmax(s, axis=-1)
        return jnp.einsum('bhqk,bkhd->bqhd', p.astype(v.dtype), v)

    out = lax.map(one_block, (jnp.arange(nb), q_blocks, c_blocks))
    return out.transpose(1, 0, 2, 3, 4).reshape(B, S, H * Dh)

def rwkv7_scan(r, log_w, k, v, a, kk):
    B, S, H, N = r.shape

    def step(state, inp):
        r_t, lw_t, k_t, v_t, a_t, kk_t = inp
        s_kk = jnp.einsum('bhvk,bhk->bhv', state, kk_t)
        state = (state * jnp.exp(lw_t)[:, :, None, :]
                 - s_kk[..., None] * (kk_t * a_t)[:, :, None, :]
                 + v_t[..., None] * k_t[:, :, None, :])
        y_t = jnp.einsum('bhvk,bhk->bhv', state, r_t)
        return state, y_t

    xs = tuple(t.transpose(1, 0, 2, 3) for t in (r, log_w, k, v, a, kk))
    state0 = jnp.zeros((B, H, N, N), jnp.float32)
    _, y = lax.scan(step, state0, xs)
    return y.transpose(1, 0, 2, 3)

def fox_rwkv_layer(x, norm_g, w_in, b_f, shift_mu, w0, w_decay_up, a0, w_iclr_up,
                   w_gate_up, k_k, k_a, r_k, gn_w, gn_b, w_out):
    B, S, _ = x.shape
    f32 = jnp.float32
    h = rmsnorm(x, norm_g)
    p = h @ w_in
    fa = p[..., :FOX_COLS]
    rw = p[..., FOX_COLS:].astype(f32)

    q, k, v, f_logit = jnp.split(fa, [FOX_WIDTH, 2 * FOX_WIDTH, 3 * FOX_WIDTH], axis=-1)
    log_f = jax.nn.log_sigmoid(f_logit.astype(f32) + b_f.astype(f32))
    hs = (B, S, FOX_HEADS, FOX_HEAD_DIM)
    o_a = forgetting_attention(q.reshape(hs), k.reshape(hs), v.reshape(hs), log_f)

    rw = rw + (token_shift(rw) - rw) * shift_mu.astype(f32)
    r, kb, vb, wd, ad, gd = jnp.split(
        rw, [RWKV_WIDTH, 2 * RWKV_WIDTH, 3 * RWKV_WIDTH,
             3 * RWKV_WIDTH + DECAY_RANK, 3 * RWKV_WIDTH + DECAY_RANK + ICLR_RANK], axis=-1)
    log_w = -jnp.exp(-jax.nn.softplus(-(w0.astype(f32) + jnp.tanh(wd) @ w_decay_up.astype(f32))) - 0.5)
    a = jax.nn.sigmoid(a0.astype(f32) + ad @ w_iclr_up.astype(f32))
    g = jax.nn.sigmoid(gd) @ w_gate_up.astype(f32)
    hr = (B, S, RWKV_HEADS, RWKV_HEAD_DIM)
    kk = (kb * k_k.astype(f32)).reshape(hr)
    kk = kk / jnp.maximum(jnp.sqrt(jnp.sum(kk * kk, axis=-1, keepdims=True)), 1e-12)
    kb = kb * (1.0 + (a - 1.0) * k_a.astype(f32))
    r_h, k_h, v_h = r.reshape(hr), kb.reshape(hr), vb.reshape(hr)
    y = rwkv7_scan(r_h, log_w.reshape(hr), k_h, v_h, a.reshape(hr), kk)
    mu = jnp.mean(y, axis=-1, keepdims=True)
    var = jnp.mean(jnp.square(y - mu), axis=-1, keepdims=True)
    y = ((y - mu) * lax.rsqrt(var + GN_EPS) * gn_w.astype(f32).reshape(RWKV_HEADS, RWKV_HEAD_DIM)
         + gn_b.astype(f32).reshape(RWKV_HEADS, RWKV_HEAD_DIM))
    y = y + jnp.sum(r_h * k_h * r_k.astype(f32), axis=-1, keepdims=True) * v_h
    o_b = (y.reshape(B, S, RWKV_WIDTH) * g).astype(x.dtype)

    mixed = jnp.concatenate([o_a.astype(x.dtype), o_b], axis=-1)
    return x + mixed @ w_out

def pool_layer(x, norm_g, w_pool, pool_scale):
    B, S, D = x.shape
    h = rmsnorm(x, norm_g).astype(jnp.float32).reshape(B, S, POOL_GROUPS, POOL_GROUP_DIM)
    cs = jnp.pad(jnp.cumsum(h, axis=1), ((0, 0), (1, 0), (0, 0), (0, 0)))
    t = jnp.arange(S)
    win = jnp.array(POOL_WINDOWS, dtype=jnp.int32)
    lo = jnp.maximum(t[:, None] + 1 - win[None, :], 0)
    grp = jnp.arange(POOL_GROUPS)[None, :]
    window_sum = cs[:, 1:] - cs[:, lo, grp]
    count = jnp.minimum(t[:, None] + 1, win[None, :]).astype(jnp.float32)
    pooled = window_sum / count[None, :, :, None] - h
    y = jnp.einsum('bsgc,gcd->bsgd', pooled.astype(x.dtype), w_pool).reshape(B, S, D)
    return x + y * pool_scale

def conv_ffn(x, norm_g, w_up, conv_w, conv_b, w_down):
    h = rmsnorm(x, norm_g)
    u = h @ w_up
    C = u.shape[-1]
    u = lax.conv_general_dilated(
        u, conv_w[:, None, :].astype(u.dtype), window_strides=(1,),
        padding=[(CONV_WIDTH - 1, 0)], dimension_numbers=('NWC', 'WIO', 'NWC'),
        feature_group_count=C) + conv_b
    gate, val = jnp.split(u, 2, axis=-1)
    return x + (jax.nn.silu(gate) * val) @ w_down

def setup_inputs(seed: int = 0) -> dict:
    key = jax.random.key(seed)
    ks = iter(jax.random.split(key, 32))
    f32 = jnp.float32

    def nrm(shape, scale):
        return jax.random.normal(next(ks), shape, f32) * scale

    def uni(shape, lo, hi):
        return jax.random.uniform(next(ks), shape, f32, lo, hi)

    E, O, L, D = N_EVEN, N_ODD, DEPTH, D_MODEL
    return {
        'x': nrm((BATCH, SEQ, D), 1.0),
        'mix_norm': 1.0 + nrm((E, D), 0.02),
        'w_in': nrm((E, D, IN_COLS), D ** -0.5),
        'b_f': uni((E, FOX_HEADS), 1.0, 6.0),
        'shift_mu': uni((E, RWKV_COLS), 0.0, 1.0),
        'w0': uni((E, RWKV_WIDTH), -6.0, -1.0),
        'w_decay_up': nrm((E, DECAY_RANK, RWKV_WIDTH), 0.1 * DECAY_RANK ** -0.5),
        'a0': nrm((E, RWKV_WIDTH), 0.1),
        'w_iclr_up': nrm((E, ICLR_RANK, RWKV_WIDTH), ICLR_RANK ** -0.5),
        'w_gate_up': nrm((E, GATE_RANK, RWKV_WIDTH), GATE_RANK ** -0.5),
        'k_k': 0.85 + nrm((E, RWKV_WIDTH), 0.02),
        'k_a': 1.0 + nrm((E, RWKV_WIDTH), 0.02),
        'r_k': nrm((E, RWKV_HEADS, RWKV_HEAD_DIM), 0.1),
        'gn_w': 1.0 + nrm((E, RWKV_WIDTH), 0.02),
        'gn_b': nrm((E, RWKV_WIDTH), 0.02),
        'w_out': nrm((E, D, D), D ** -0.5),
        'pool_norm': 1.0 + nrm((O, D), 0.02),
        'w_pool': nrm((O, POOL_GROUPS, POOL_GROUP_DIM, POOL_GROUP_DIM), POOL_GROUP_DIM ** -0.5),
        'pool_scale': uni((O, D), 0.5, 1.0),
        'ffn_norm': 1.0 + nrm((L, D), 0.02),
        'w_ffn_up': nrm((L, D, 2 * D_FF), D ** -0.5),
        'conv_w': nrm((L, CONV_WIDTH, 2 * D_FF), CONV_WIDTH ** -0.5),
        'conv_b': nrm((L, 2 * D_FF), 0.02),
        'w_ffn_down': nrm((L, D_FF, D), D_FF ** -0.5),
        'final_norm': 1.0 + nrm((D,), 0.02),
    }

def reference(x, mix_norm, w_in, b_f, shift_mu, w0, w_decay_up, a0, w_iclr_up, w_gate_up,
              k_k, k_a, r_k, gn_w, gn_b, w_out, pool_norm, w_pool, pool_scale,
              ffn_norm, w_ffn_up, conv_w, conv_b, w_ffn_down, final_norm):
    e = 0
    o = 0
    for layer in range(DEPTH):
        if layer % 2 == 0:
            x = fox_rwkv_layer(x, mix_norm[e], w_in[e], b_f[e], shift_mu[e], w0[e],
                               w_decay_up[e], a0[e], w_iclr_up[e], w_gate_up[e],
                               k_k[e], k_a[e], r_k[e], gn_w[e], gn_b[e], w_out[e])
            e += 1
        else:
            x = pool_layer(x, pool_norm[o], w_pool[o], pool_scale[o])
            o += 1
        x = conv_ffn(x, ffn_norm[layer], w_ffn_up[layer], conv_w[layer], conv_b[layer],
                     w_ffn_down[layer])
    return rmsnorm(x, final_norm)


_drawn_inputs = setup_inputs


def setup_inputs(seed=0):
    import zlib

    import numpy as np

    out = dict(_drawn_inputs(seed))
    spreads = {}
    factors = {'mix_norm': 3.088,
     'w_decay_up': 37.473,
     'a0': 3.545,
     'k_k': 64.0,
     'k_a': 6.352,
     'gn_w': 51.752,
     'gn_b': 59.472,
     'pool_norm': 46.256,
     'ffn_norm': 11.438,
     'conv_b': 11.661,
     'final_norm': 8.057}
    for name, (base, spread) in spreads.items():
        noise = np.random.default_rng([zlib.crc32(name.encode()), seed]).standard_normal(out[name].shape)
        drawn = base * np.exp(spread * noise) if base else spread * noise
        out[name] = jnp.asarray(drawn.astype(out[name].dtype))
    for name, factor in factors.items():
        out[name] = (out[name] * factor).astype(out[name].dtype)
    return out
```

```python
from contextlib import ExitStack, contextmanager

import concourse.bass as bass
from concourse import mybir

F32 = mybir.dt.float32
F32R = mybir.dt.float32r
U8 = mybir.dt.uint8
ALU = mybir.AluOpType
ACT = mybir.ActivationFunctionType
AX = mybir.AxisListType

P = 128
T = 256
D = 2048
DC = D // P
HEADS = 8
PAIRS = 8
LORA = 96
D_FF = 5632
QUARTERS = 4
FC = D_FF // P // QUARTERS
RMS_EPS = 1e-6
GN_EPS = 64e-5
EXP_HALF = 0.6065306597126334
ATT_SCALE = P ** -0.5
SLOTS = 4
UA = 8 * P
UB = FC * P
LEVELS = 6

MU_R, MU_K, MU_V, W0, A0, K_K, K_A, R_K, GN_W, GN_B = range(10)
ONE_LOW, ONE_UP, IDENT, HEAD_BLOCKS, CAUSAL, MASKS = 6, 7, 8, 9, 10, 11
G_LOW, G_RW, G_FOX, G_OUT = 2, 2 * PAIRS, HEADS, DC // 2
G_UP, G_DOWN, G_POOL = FC, DC // SLOTS, 2
G_QUARTER = G_UP + G_DOWN
FIRST_RW = G_LOW
FIRST_FOX = FIRST_RW + G_RW
FIRST_OUT = FIRST_FOX + G_FOX
FIRST_FFN0 = FIRST_OUT + G_OUT
FIRST_POOL = FIRST_FFN0 + QUARTERS * G_QUARTER
FIRST_FFN1 = FIRST_POOL + G_POOL
FIRST_FFN = (FIRST_FFN0, FIRST_FFN1)
R_QUARTER = 2 * G_UP + 4 * G_DOWN
R_POOL = 2 * FIRST_FFN0 + QUARTERS * R_QUARTER
R_FFN = (2 * FIRST_FFN0, R_POOL + DC)


class Chain:

    def __init__(self, eng, sem):
        self.eng, self.sem, self.base, self.k = eng, sem, 0, 0

    def link(self, ins):
        self.k += 1
        ins.then_inc(self.sem, 1)
        self.eng.wait_ge(self.sem, self.base + self.k)

    def mark(self, ins):
        self.k += 1
        ins.then_inc(self.sem, 1)
        return self.base + self.k

    def done(self, count):
        self.eng.wait_ge(self.sem, count)

    @contextmanager
    def loop(self, count, per, start=0):
        base = self.base + self.k
        with self.eng.Fori(start, count) as i:
            self.base, self.k = per * i + (base - per * start), 0
            yield i
            assert self.k == per, (self.k, per)
        self.base, self.k = base + per * (count - start), 0


def chunk(t, c, lo=0, hi=T):
    return t[:, bass.ds(c, 1), lo:hi].rearrange("p o t -> p (o t)")


def trunk(nc, x_in, gains, wa, wb, mix_p, mu0, b_f, lora, conv_p, pool_p, mats, inv_count, out):
    with ExitStack() as ctx:
        def sb(name, shape, dt=F32):
            return ctx.enter_context(nc.sbuf_tensor(name, shape, dt))

        def sem(name):
            return ctx.enter_context(nc.semaphore(name))

        x = sb("x", [P, DC, T])
        h = sb("h", [P, DC, 2 * T], F32R)
        w_raw = sb("w_raw", [P, SLOTS, UB])
        w_hi = sb("w_hi", [P, SLOTS, UB], F32R)
        w_lo = sb("w_lo", [P, SLOTS, UB], F32R)
        gain = sb("gain", [P, 5, DC])
        mixp = sb("mixp", [P, PAIRS, 10])
        mu_low = sb("mu_low", [P, 4])
        bf = sb("bf", [P, 1])
        convp = sb("convp", [P, 2 * 2 * FC * QUARTERS, 4])
        poolp = sb("poolp", [P, DC])
        mask = sb("mask", [P, 2, 3 * P], U8)
        mat = sb("mat", [P, 14, P])
        ones = sb("ones", [P, P])
        sq = sb("sq", [P, T])
        ssum = sb("ssum", [P, T])
        ms = sb("ms", [P, T])
        rstd = sb("rstd", [P, T])
        tmp = sb("tmp", [P, T])
        cross = sb("cross", [P, 2, T])
        e_pad = sb("e_pad", [P, 2, 2 + T])
        forget = sb("forget", [P, 2, T])
        fox_k = sb("fox_k", [P, HEADS, T])
        rwkv_out = sb("rwkv_out", [P, PAIRS, T])

        scope = ExitStack()

        def shared(name, shape, dt=F32):
            return scope.enter_context(nc.sbuf_tensor(name, shape, dt))

        low = shared("low", [P, 4, T])
        lora_w = shared("lora_w", [P, 4, P])
        rkv = shared("rkv", [P, 3, T])
        gate = shared("gate", [P, T])
        iclr = shared("iclr", [P, T])
        log_w = shared("log_w", [P, T])
        kk = shared("kk", [P, T])
        kn = shared("kn", [P, T])
        rs = shared("rs", [P, T])
        bonus = shared("bonus", [P, T])
        cum = shared("cum", [P, 2, P + 1])
        neg_mid = shared("neg_mid", [P, 2])
        dec = shared("dec", [P, 2, P + 1])
        inv_dec = shared("inv_dec", [P, 2, P + 1])
        kr = shared("kr", [P, 2, 2 * P])
        kinv = shared("kinv", [P, 2, P])
        binv = shared("binv", [P, 2, P])
        tok = shared("tok", [P, 4, P])
        akr = shared("akr", [P, 4, 2 * P])
        abr = shared("abr", [P, 4, 2 * P])
        al = shared("al", [P, 4, P])
        inv = shared("inv", [P, 2, 4, P])
        off = shared("off", [P, 4, P])
        w1 = shared("w1", [P, 4, P])
        ru = shared("ru", [P, 2, P])
        state = shared("state", [P, P])
        state_scale = shared("state_scale", [P, 1])
        y = shared("y", [P, T])
        y_sq = shared("y_sq", [P, T])
        var = shared("var", [P, T])
        scope.close()
        act_in = sb("act_in", [P, DC, 2 * T], F32R)
        forget_row = shared("forget_row", [1, HEADS * T])
        qv = shared("qv", [P, 2, T])
        prob = shared("prob", [P, 3 * P])
        row_max = shared("row_max", [P, 2])
        row_sum = shared("row_sum", [P, 2])
        prob_t = shared("prob_t", [P, 3 * P])
        v_tok = shared("v_tok", [P, 2, P])
        mix_t = shared("mix_t", [P, T])
        scope.close()
        u_t = sb("u_t", [P, 4, T])
        invc = sb("invc", [P, 4, T])
        win = sb("win", [P, 3, 16 + T])

        acc = [ctx.enter_context(nc.psum_tensor(f"acc{b}", [P, 512], F32)) for b in range(2)]
        aux = ctx.enter_context(nc.psum_tensor("aux", [P, 6, 512], F32))

        params_landed = sem("params_landed")
        x_landed = sem("x_landed")
        w_landed = [sem(f"w_landed{s}") for s in range(SLOTS)]
        names = {}

        def S(name):
            if name not in names:
                names[name] = sem(name)
            return names[name]

        hi_ready, lo_ready, units_done = S("hi_ready"), S("lo_ready"), S("units_done")
        acc_free = S("acc_free")
        x_done = S("x_chunks_final")

        def mat_b(k, n):
            return mat[:, k:k + 1, :].to_broadcast([P, n, P])

        block = ctx.enter_context(nc.Block())

        @block.sync
        def _(sp):
            sp.dma_start(x[:], x_in).then_inc(x_landed, 16)
            sp.dma_start(gain[:], gains).then_inc(params_landed, 16)
            for s in range(SLOTS):
                sp.dma_start(w_raw[:, s, 0:UA], wa[s]).then_inc(w_landed[s], 16)
            for dst, src in ((mixp, mix_p), (mu_low, mu0), (bf, b_f), (mat, mats), (convp, conv_p),
                             (poolp, pool_p)):
                sp.dma_start(dst[:], src).then_inc(params_landed, 16)

            def load(w, first, g, n, cols):
                with sp.Fori(0, n) as i:
                    for s in range(SLOTS):
                        sp.wait_ge(lo_ready, 4 * i + (4 * g + s - 3))
                        src = w[bass.ds(4 * i + (4 * first + s), 1)].rearrange("o p c -> (o p) c")
                        sp.dma_start(w_raw[:, s, 0:cols], src).then_inc(w_landed[s], 16)

            load(wa, 1, 1, FIRST_FFN0 - 1, UA)
            sp.wait_ge(S("mixed_ready"), PAIRS + HEADS)
            sp.dma_start(invc[:], inv_count).then_inc(S("counts_landed"), 16)
            g, a, b = FIRST_FFN0, FIRST_FFN0, 0
            for layer in range(2):
                for q in range(QUARTERS):
                    load(wa, a, g, G_UP, UA)
                    load(wb, b, g + G_UP, G_DOWN, UB)
                    g, a, b = g + G_QUARTER, a + G_UP, b + G_DOWN
                if layer == 0:
                    load(wa, a, g, G_POOL, UA)
                    g, a = g + G_POOL, a + G_POOL
            sp.wait_ge(S("out_ready"), DC)
            sp.dma_start(out, x[:]).then_inc(S("out_stored"), 16)
            sp.wait_ge(S("out_stored"), 16)

        @block.gpsimd
        def _(pool):
            consts = S("consts_ready")
            for t, v in ((ones, 1.0), (e_pad, 0.0), (cum, 0.0), (akr, 0.0),
                         (abr, 0.0), (al, 0.0)):
                nc.gpsimd.memset(t[:], v).then_inc(consts, 1)
            pool.wait_ge(consts, N_CONSTS)

            def norm(n):
                if n == 0:
                    pool.wait_ge(x_landed, 16)
                else:
                    pool.wait_ge(S("mean_square_ready"), n)
                nc.gpsimd.memset(ssum[:], 0.0).then_inc(S("sum_cleared"), 1)
                pool.wait_ge(S("sum_cleared"), n + 1)
                with pool.Fori(0, DC) as c:
                    if n:
                        pool.wait_ge(x_done, c + (DC * (n - 1) + 1))
                    nc.gpsimd.tensor_tensor(sq[:], chunk(x, c), chunk(x, c), ALU.mult).then_inc(S("squared"), 1)
                    pool.wait_ge(S("squared"), c + (DC * n + 1))
                    nc.gpsimd.tensor_tensor(ssum[:], ssum[:], sq[:], ALU.add).then_inc(S("summed"), 1)
                    pool.wait_ge(S("summed"), c + (DC * n + 1))

            norm(0)
            with pool.Fori(0, PAIRS) as j:
                pool.wait_ge(S("grams_masked"), j + 1)
                for lv in range(LEVELS):
                    if lv:
                        pool.wait_ge(S("w1_ps"), LEVELS * j + lv)
                    nc.gpsimd.tensor_tensor(off[:], al[:], mat_b(lv, 4), ALU.mult).then_inc(S("off_ready"), 1)
            for n in range(1, 5):
                norm(n)

        @block.scalar
        def _(act):
            def hi(g, s, cols):
                act.wait_ge(w_landed[s], 16 * g + 32)
                act.wait_ge(units_done, 4 * g + (s + 1))
                nc.scalar.activation(w_hi[:, s, 0:cols], w_raw[:, s, 0:cols], ACT.Copy).then_inc(hi_ready, 1)

            def cross_half(bank, done):
                act.wait_ge(units_done, done)
                nc.scalar.activation(cross[:, bank], acc[bank][:, T:2 * T], ACT.Copy).then_inc(S("cross_ready"), 1)

            def tile(g, e, cols):
                hi(g, 2 * e, cols)
                hi(g, 2 * e + 1, cols)
                cross_half(e, 4 * g + (2 * e + 2))

            def root(n):
                act.wait_ge(S("mean_square_ready"), n + 1)
                nc.scalar.activation(ms[:], ms[:], ACT.Sqrt).then_inc(S("rms_ready"), 1)

            def next_h(which, c, n):
                act.wait_ge(x_done, n)
                nc.scalar.activation(chunk(h, c), chunk(x, c), ACT.Copy,
                                     scale=gain[:, which, bass.ds(c, 1)]).then_inc(S("h_hi_ready"), 1)

            act.dma_start(lora_w[:], lora[0]).then_inc(S("lora_landed"), 16)
            act.wait_ge(x_landed, 16)
            act.wait_ge(params_landed, 16 * N_PARAMS)
            for s in range(SLOTS):
                act.wait_ge(w_landed[s], 16)
                nc.scalar.activation(w_hi[:, s, 0:UA], w_raw[:, s, 0:UA], ACT.Copy).then_inc(hi_ready, 1)
            with act.Fori(0, DC) as c:
                nc.scalar.activation(chunk(h, c), chunk(x, c), ACT.Copy,
                                     scale=gain[:, 0, bass.ds(c, 1)]).then_inc(S("h_hi_ready"), 1)
            root(0)
            for g in range(G_LOW):
                for e in range(2):
                    tile(g, e, UA)
            act.wait_ge(S("low_shifted"), 1)
            nc.scalar.activation(low[0:LORA, 1], low[0:LORA, 1], ACT.Tanh).then_inc(S("low_tanh"), 1)
            nc.scalar.activation(low[:, 2:4], low[:, 2:4], ACT.Tanh, scale=0.5).then_inc(S("low_tanh"), 1)
            act.wait_ge(S("forget_abs"), 1)
            fg = forget[LORA:LORA + HEADS, 1]
            nc.scalar.activation(fg, fg, ACT.Exp, scale=-1.0).then_inc(S("forget_exp"), 1)
            act.wait_ge(S("forget_exp"), 1)
            nc.scalar.activation(fg, fg, ACT.Ln, bias=ones[LORA:LORA + HEADS, 0:1]).then_inc(S("forget_ln"), 1)

            def rwkv(j):
                par = lambda k: mixp[:, bass.ds(j, 1), k]
                act.wait_ge(S("lora_ps"), j + 1)
                act.dma_start(lora_w[:], lora[bass.ds(j + 1, 1)].rearrange("o p a b -> (o p) a b")) \
                    .then_inc(S("lora_landed"), 16)
                nc.scalar.activation(iclr[:], aux[:, 0, 0:T], ACT.Tanh, scale=0.5, bias=par(A0))
                nc.scalar.activation(log_w[:], aux[:, 0, T:2 * T], ACT.Tanh, scale=0.5, bias=par(W0))
                nc.scalar.activation(gate[:], aux[:, 1, 0:T], ACT.Copy).then_inc(S("lora_read"), 1)
                act.wait_ge(S("key_norm_ready"), j + 1)
                nc.scalar.activation(rs[:], rs[:], ACT.Sqrt).then_inc(S("key_root_ready"), 1)
                act.wait_ge(S("cum_ready"), j + 1)
                for c in range(2):
                    nc.scalar.activation(dec[:, c], cum[:, c], ACT.Exp, bias=neg_mid[:, c:c + 1])
                for c in range(2):
                    ins = nc.scalar.activation(inv_dec[:, c], cum[:, c], ACT.Exp, scale=-1.0,
                                               bias=cum[:, c, P // 2:P // 2 + 1])
                ins.then_inc(S("decay_ready"), 1)
                act.wait_ge(S("turned_ps"), j + 1)
                nc.scalar.activation(tok[:], aux[:, 4].rearrange("p (a b) -> p a b", a=4), ACT.Copy) \
                    .then_inc(S("tok_ready"), 1)
                for lv in range(LEVELS):
                    act.wait_ge(S("w1_ps"), LEVELS * j + (lv + 1))
                    nc.scalar.activation(w1[:], aux[:, 0].rearrange("p (a b) -> p a b", a=4), ACT.Copy) \
                        .then_inc(S("w1_ready"), 1)
                for k in range(4):
                    act.wait_ge(S("ru_ps"), 4 * j + (k + 1))
                    nc.scalar.activation(ru[:, k % 2], aux[:, 1, 0:P], ACT.Copy).then_inc(S("ru_ready"), 1)
                act.wait_ge(S("y_ps"), j + 1)
                nc.scalar.activation(y[:], aux[:, 5, 0:T], ACT.Copy).then_inc(S("y_ready"), 1)
                act.wait_ge(S("y_centred"), j + 1)
                nc.scalar.activation(y_sq[:], y[:], ACT.Square).then_inc(S("y_squared"), 1)
                act.wait_ge(S("var_ready"), j + 1)
                nc.scalar.activation(var[:], var[:], ACT.Sqrt).then_inc(S("group_root_ready"), 1)
                act.wait_ge(S("y_scaled"), j + 1)
                nc.scalar.activation(y[:], y[:], ACT.Identity, scale=par(GN_W), bias=par(GN_B)) \
                    .then_inc(S("group_norm_ready"), 1)

            act.wait_ge(S("halved"), 1)
            with act.Fori(0, PAIRS) as j:
                for e in range(2):
                    for t in range(2):
                        tile(2 * j + (FIRST_RW + e), t, UA)
                rwkv(j)

            act.wait_ge(S("forget_ready"), 1)
            act.wait_ge(S("rwkv_done"), PAIRS)
            act.wait_ge(S("lora_landed"), 16 * (PAIRS + 1))
            act.dma_start(forget_row[0:1, :].rearrange("o (h t) -> o h t", t=T),
                          forget[LORA:LORA + HEADS, 0]).then_inc(S("forget_row_landed"), 16)

            def fox(n):
                act.wait_ge(S("scores_ready"), n + 1)
                nc.scalar.activation(prob[:, 0:P], prob[:, 0:P], ACT.Exp, scale=ATT_SCALE, bias=row_max[:, 0:1],
                                     accum_out=row_sum[:, 0:1])
                nc.scalar.activation(prob[:, P:3 * P], prob[:, P:3 * P], ACT.Exp, scale=ATT_SCALE,
                                     bias=row_max[:, 1:2], accum_out=row_sum[:, 1:2]).then_inc(S("exp_ready"), 1)
                act.wait_ge(S("fox_turned_ps"), n + 1)
                nc.scalar.activation(prob_t[:], aux[:, 1, 0:3 * P], ACT.Copy)
                nc.scalar.activation(v_tok[:], aux[:, 2, 0:T].rearrange("p (a b) -> p a b", a=2), ACT.Copy) \
                    .then_inc(S("fox_turned"), 1)

            with act.Fori(0, HEADS) as n:
                for t in range(2):
                    tile(n + FIRST_FOX, t, UA)
                fox(n)

            def out_group(i, cols=UA):
                for e in range(2):
                    tile(i + FIRST_OUT, e, cols)
                    next_h(2, 2 * i + e, 2 * i + (e + 1))

            with act.Fori(0, G_OUT) as i:
                out_group(i)

            def feature_hi(pair, c):
                act.wait_ge(S("product_ready"), pair + 1)
                nc.scalar.activation(chunk(act_in, c), u_t[:, 3], ACT.Copy).then_inc(S("feature_hi_ready"), 1)

            def tap(pair, conv, e):
                act.wait_ge(S("scaled_ready"), 2 * pair + (e + 1))
                par = lambda k: convp[:, bass.ds(conv + e, 1), k]
                nc.scalar.activation(u_t[:, e], e_pad[:, e, 2:], ACT.Identity, scale=par(2), bias=par(3)) \
                    .then_inc(S("tap_ready"), 1)

            def up_pair(g, pair, c, conv, cols, first=False):
                tile(g, 0, cols)
                if not first:
                    feature_hi(pair - 1, c - 1)
                tap(pair, conv, 0)
                tile(g, 1, cols)
                act.wait_ge(S("gate_ready"), pair + 1)
                nc.scalar.activation(u_t[:, 2], u_t[:, 0], ACT.Tanh, scale=0.5).then_inc(S("tanh_ready"), 1)
                tap(pair, conv, 1)

            for layer in range(2):
                g0, p0 = FIRST_FFN[layer], layer * QUARTERS * G_UP
                for q in range(QUARTERS):
                    if q == 0:
                        root(1 + 2 * layer)
                    up_pair(g0, p0, 0, 2 * p0, UA, first=True)
                    with act.Fori(1, G_UP - 1) as i:
                        up_pair(i + g0, i + p0, i, 2 * i + 2 * p0, UA)
                    last = G_UP - 1
                    up_pair(g0 + last, p0 + last, last, 2 * (p0 + last), UB)
                    feature_hi(p0 + last, last)
                    with act.Fori(0, G_DOWN - 1) as i:
                        for s in range(SLOTS):
                            hi(i + (g0 + G_UP), s, UB)
                            cross_half(s % 2, 4 * i + (4 * (g0 + G_UP) + s + 1))
                    for s in range(SLOTS):
                        if not (layer == 1 and q == QUARTERS - 1):
                            hi(g0 + G_QUARTER - 1, s, UA)
                        cross_half(s % 2, 4 * (g0 + G_QUARTER - 1) + s + 1)
                    g0, p0 = g0 + G_QUARTER, p0 + G_UP
                if layer == 0:
                    root(2)
                    for i in range(G_POOL):
                        for s in range(SLOTS):
                            hi(FIRST_POOL + i, s, UA)
                            for r in range(2):
                                cross_half(r, 4 * (FIRST_POOL + i) + s + 1)
                            for r in range(2):
                                c = 8 * i + 2 * s + r
                                next_h(3, c, 2 * DC + c + 1)
            root(4)

        @block.vector
        def _(dve):
            own = Chain(dve, S("dve_own"))
            tt, ts, stt = nc.vector.tensor_tensor, nc.vector.tensor_scalar, nc.vector.scalar_tensor_tensor
            dve.sem_inc(acc_free, 2)

            def lo(g, s, cols):
                dve.wait_ge(hi_ready, 4 * g + (s + 5))
                tt(w_lo[:, s, 0:cols], w_raw[:, s, 0:cols], w_hi[:, s, 0:cols].bitcast(F32), ALU.subtract) \
                    .then_inc(lo_ready, 1)

            def read_result(bank, n):
                dve.wait_ge(S("cross_ready"), n + 1)
                tt(tmp[:], acc[bank][:, 0:T], cross[:, bank], ALU.add).then_inc(acc_free, 1)
                dve.wait_ge(acc_free, n + 3)

            def scaled_result(b, bank, n):
                read_result(bank, n)
                own.link(tt(e_pad[:, b, 2:], tmp[:], rstd[:], ALU.mult))

            def shifted(dst, b, mu, rows=P):
                e, before = e_pad[0:rows, b, 2:], e_pad[0:rows, b, 1:1 + T]
                own.link(tt(tmp[0:rows], before, e, ALU.subtract))
                return stt(out=dst, in0=tmp[0:rows], scalar=mu, in1=e, op0=ALU.mult, op1=ALU.add)

            def split(dst, c, src):
                own.link(nc.vector.tensor_copy(chunk(dst, c), src))
                return tt(chunk(dst, c, T, 2 * T), src, chunk(dst, c).bitcast(F32), ALU.subtract)

            def next_h(which, c, n):
                dve.wait_ge(S("h_hi_ready"), n)
                stt(out=chunk(h, c, T, 2 * T), in0=chunk(x, c), scalar=gain[:, which, bass.ds(c, 1)],
                    in1=chunk(h, c).bitcast(F32), op0=ALU.mult, op1=ALU.subtract).then_inc(S("h_ready"), 1)

            def mean_square(n):
                dve.wait_ge(S("square_sum_ps"), n + 1)
                ts(ms[:], aux[:, 4, 0:T], 1.0 / D, RMS_EPS, ALU.mult, ALU.add).then_inc(S("mean_square_ready"), 1)
                dve.wait_ge(S("rms_ready"), n + 1)
                nc.vector.reciprocal(rstd[:], ms[:]).then_inc(S("rstd_ready"), 1)
                dve.wait_ge(S("rstd_ready"), n + 1)

            dve.wait_ge(params_landed, 16 * N_PARAMS)
            dve.wait_ge(S("consts_ready"), N_CONSTS)
            for s in range(SLOTS):
                lo(-1, s, UA)
            for c in range(2):
                own.link(nc.vector.tensor_copy(mask[:, c].rearrange("p (a b) -> p a b", a=3), mat[:, MASKS:MASKS + 3]))
            ts(mixp[:, :, W0:A0 + 1], mixp[:, :, W0:A0 + 1], 0.5, None, ALU.mult).then_inc(S("halved"), 1)
            with dve.Fori(0, DC) as c:
                next_h(0, c, c + 1)
            mean_square(0)
            for g in range(G_LOW):
                for e in range(2):
                    n = 2 * g + e
                    lo(g, 2 * e, UA)
                    lo(g, 2 * e + 1, UA)
                    if n == 0:
                        dve.wait_ge(S("rstd_ready"), 1)
                    scaled_result(e, n % 2, n)
                    if n == 0:
                        rows = slice(LORA, LORA + HEADS)
                        fx, fm = forget[rows, 0], forget[rows, 1]
                        own.link(ts(fx, e_pad[rows, 0, 2:], bf[rows, 0:1], None, ALU.add))
                        stt(out=fm, in0=fx, scalar=-1.0, in1=fx, op0=ALU.mult, op1=ALU.max) \
                            .then_inc(S("forget_abs"), 1)
                    rows = LORA if n < 2 else P
                    ins = shifted(low[0:rows, n], e, mu_low[0:rows, n:n + 1], rows)
                    if n < 3:
                        own.link(ins)
                    else:
                        ins.then_inc(S("low_shifted"), 1)
            dve.wait_ge(S("low_tanh"), 2)
            ts(low[:, 2:4], low[:, 2:4], 0.5, 0.5, ALU.mult, ALU.add).then_inc(S("low_ready"), 1)
            dve.wait_ge(S("forget_ln"), 1)
            rows = slice(LORA, LORA + HEADS)
            own.link(stt(out=forget[rows, 0], in0=forget[rows, 0], scalar=0.0, in1=forget[rows, 1], op0=ALU.min,
                         op1=ALU.subtract))
            own.link(nc.vector.tensor_tensor_scan(forget[rows, 1], ones[rows, 0:1].to_broadcast([HEADS, T]), forget[rows, 0], 0.0, ALU.mult,
                                                  ALU.add))
            ts(forget[rows, 0], forget[rows, 1], -1.0 / ATT_SCALE, None, ALU.mult).then_inc(S("forget_ready"), 1)

            def rwkv(j):
                par = lambda k: mixp[:, bass.ds(j, 1), k]
                r, k, v = rkv[:, 0], rkv[:, 1], rkv[:, 2]
                dve.wait_ge(S("lora_read"), j + 1)
                own.link(ts(iclr[:], iclr[:], 0.5, 0.5, ALU.mult, ALU.add))
                own.link(ts(log_w[:], log_w[:], -EXP_HALF / 2, -EXP_HALF / 2, ALU.mult, ALU.add))
                for c in range(2):
                    own.link(nc.vector.tensor_tensor_scan(cum[:, c, 1:], ones[:], log_w[:, c * P:c * P + P],
                                                          0.0, ALU.mult, ALU.add))
                ts(neg_mid[:], cum[:, :, P // 2], -1.0, None, ALU.mult).then_inc(S("cum_ready"), 1)
                own.link(ts(kk[:], k, par(K_K), None, ALU.mult))
                tt(kn[:], kk[:], kk[:], ALU.mult).then_inc(S("key_squared"), 1)
                dve.wait_ge(S("key_norm_ps"), j + 1)
                ts(rs[:], aux[:, 2, 0:T], 1e-24, None, ALU.max).then_inc(S("key_norm_ready"), 1)
                own.link(ts(y[:], iclr[:], 1.0, par(K_A), ALU.subtract, ALU.mult))
                own.link(stt(out=k, in0=y[:], scalar=1.0, in1=k, op0=ALU.add, op1=ALU.mult))
                stt(out=y_sq[:], in0=r, scalar=par(R_K), in1=k, op0=ALU.mult, op1=ALU.mult) \
                    .then_inc(S("bonus_product"), 1)
                dve.wait_ge(S("key_root_ready"), j + 1)
                own.link(nc.vector.reciprocal(rs[:], rs[:]))
                own.link(tt(kk[:], kk[:], rs[:], ALU.mult))
                own.link(stt(out=kn[:], in0=kk[:], scalar=-1.0, in1=iclr[:], op0=ALU.mult, op1=ALU.mult))
                halves = lambda t: t.rearrange("p (a b) -> p a b", a=2)
                dve.wait_ge(S("decay_ready"), j + 1)
                tt(kinv[:], halves(k), inv_dec[:, :, 1:], ALU.mult)
                tt(binv[:], halves(kn[:]), inv_dec[:, :, 1:], ALU.mult).then_inc(S("keys_ready"), 1)
                tt(kr[:, :, 0:P], halves(kk[:]), dec[:, :, 0:P], ALU.mult)
                tt(kr[:, :, P:2 * P], halves(r), dec[:, :, 1:], ALU.mult).then_inc(S("queries_ready"), 1)
                dve.wait_ge(S("bonus_ps"), j + 1)
                tt(bonus[:], aux[:, 3, 0:T], v, ALU.mult).then_inc(S("bonus_ready"), 1)
                dve.wait_ge(S("grams_ps"), 2 * j + 2)
                tt(state_scale[:], dec[:, 0, P:P + 1], inv_dec[:, 1, 0:1], ALU.mult)
                for hd in range(2):
                    for dst, bank in ((akr, hd), (abr, 2 + hd)):
                        nc.vector.copy_predicated(dst[:, 2 * hd:2 * hd + 2], mask[:, :, 0:2 * P],
                                                  aux[:, bank].rearrange("p (a b) -> p a b", a=2))
                    ins = nc.vector.copy_predicated(al[:, 2 * hd:2 * hd + 2], mask[:, :, 2 * P:],
                                                     aux[:, 4 + hd, 0:2 * P].rearrange("p (a b) -> p a b", a=2))
                ins.then_inc(S("grams_masked"), 1)
                dve.wait_ge(S("grams_masked"), j + 1)
                own.link(tt(inv[:, 0], abr[:, :, 0:P], mat_b(ONE_UP, 4), ALU.mult))
                own.link(tt(inv[:, 1], al[:], mat_b(ONE_LOW, 4), ALU.mult))
                tt(inv[:, 0], inv[:, 0], mat_b(IDENT, 4), ALU.add)
                tt(inv[:, 1], inv[:, 1], mat_b(IDENT, 4), ALU.add).then_inc(S("inv_ready"), 1)
                for lv in range(LEVELS):
                    dve.wait_ge(S("inv_ps"), LEVELS * j + (lv + 1))
                    dve.wait_ge(S("inv_ready"), (LEVELS + 1) * j + (lv + 1))
                    n = 2 if lv < LEVELS - 1 else 1
                    tt(inv[:, 0:n], inv[:, 0:n], aux[:, 2:2 + n].rearrange("p m (a b) -> p m a b", a=4), ALU.add) \
                        .then_inc(S("inv_ready"), 1)
                dve.wait_ge(S("state_ps"), j + 1)
                stt(out=state[:], in0=aux[:, 4, 0:P], scalar=state_scale[:], in1=mat[:, HEAD_BLOCKS], op0=ALU.mult,
                    op1=ALU.mult).then_inc(S("state_ready"), 1)
                dve.wait_ge(S("mean_ps"), j + 1)
                stt(out=y[:], in0=aux[:, 2, 0:T], scalar=-1.0 / 64, in1=y[:], op0=ALU.mult, op1=ALU.add) \
                    .then_inc(S("y_centred"), 1)
                dve.wait_ge(S("var_ps"), j + 1)
                ts(var[:], aux[:, 3, 0:T], 1.0 / 64, GN_EPS, ALU.mult, ALU.add).then_inc(S("var_ready"), 1)
                dve.wait_ge(S("group_root_ready"), j + 1)
                own.link(nc.vector.reciprocal(var[:], var[:]))
                tt(y[:], y[:], var[:], ALU.mult).then_inc(S("y_scaled"), 1)
                dve.wait_ge(S("group_norm_ready"), j + 1)
                own.link(tt(y[:], y[:], bonus[:], ALU.add))
                tt(chunk(rwkv_out, j), y[:], gate[:], ALU.mult).then_inc(S("rwkv_done"), 1)

            with own.loop(PAIRS, 25) as j:
                for e in range(2):
                    for t in range(2):
                        lo(2 * j + (FIRST_RW + e), 2 * t, UA)
                        lo(2 * j + (FIRST_RW + e), 2 * t + 1, UA)
                        n = 4 * j + (2 * FIRST_RW + 2 * e + t)
                        scaled_result(t, t, n)
                        if e == t == 0:
                            own.link(nc.vector.tensor_copy(chunk(fox_k, j), e_pad[:, 0, 2:]))
                        else:
                            m = 2 * e + t - 1
                            own.link(shifted(rkv[:, m], t, mixp[:, bass.ds(j, 1), MU_R + m]))
                rwkv(j)

            dve.wait_ge(S("rwkv_done"), PAIRS)
            dve.wait_ge(S("lora_landed"), 16 * (PAIRS + 1))
            with own.loop(PAIRS, 1) as j:
                split(act_in, j, chunk(rwkv_out, j)).then_inc(S("mixed_ready"), 1)

            def fox(n):
                dve.wait_ge(S("scores_ps"), n + 1)
                own.link(tt(prob[:, 0:P], aux[:, 0, 0:P], mat[:, CAUSAL], ALU.add))
                own.link(nc.vector.tensor_copy(prob[:, P:2 * P], aux[:, 0, P:2 * P]))
                own.link(tt(prob[:, 2 * P:], aux[:, 0, 2 * P:3 * P], mat[:, CAUSAL], ALU.add))
                nc.vector.tensor_reduce(row_max[:, 0:1], prob[:, 0:P], AX.X, ALU.max)
                own.link(nc.vector.tensor_reduce(row_max[:, 1:2], prob[:, P:], AX.X, ALU.max))
                ts(row_max[:], row_max[:], -ATT_SCALE, None, ALU.mult).then_inc(S("scores_ready"), 1)
                dve.wait_ge(S("exp_ready"), n + 1)
                own.link(nc.vector.reciprocal(row_sum[:], row_sum[:]))
                ts(prob[:, 0:P], prob[:, 0:P], row_sum[:, 0:1], None, ALU.mult)
                ts(prob[:, P:], prob[:, P:], row_sum[:, 1:2], None, ALU.mult).then_inc(S("probs_ready"), 1)
                dve.wait_ge(S("attn_ps"), n + 1)
                own.link(nc.vector.tensor_copy(mix_t[:], aux[:, 3, 0:T]))
                split(act_in, n + PAIRS, mix_t[:]).then_inc(S("mixed_ready"), 1)

            with own.loop(HEADS, 10) as n:
                for t in range(2):
                    lo(n + FIRST_FOX, 2 * t, UA)
                    lo(n + FIRST_FOX, 2 * t + 1, UA)
                    scaled_result(t, t, 2 * n + (2 * FIRST_FOX + t))
                    ins = nc.vector.tensor_copy(qv[:, t], e_pad[:, t, 2:])
                    if t == 0:
                        own.link(ins)
                    else:
                        ins.then_inc(S("qv_ready"), 1)
                fox(n)

            def add_to_x(c, bank, n, final):
                read_result(bank, n)
                ins = tt(chunk(x, c), chunk(x, c), tmp[:], ALU.add)
                if final is not None:
                    ins.then_inc(x_done, 1)
                    dve.wait_ge(x_done, final)
                else:
                    own.link(ins)

            with own.loop(G_OUT, 0) as i:
                for e in range(2):
                    lo(i + FIRST_OUT, 2 * e, UA)
                    lo(i + FIRST_OUT, 2 * e + 1, UA)
                    add_to_x(2 * i + e, e, 2 * i + (2 * FIRST_OUT + e), 2 * i + (e + 1))
                    next_h(2, 2 * i + e, 2 * i + (DC + e + 1))
            mean_square(1)

            def taps(conv, e, k):
                return stt(out=u_t[:, e], in0=e_pad[:, e, k:k + T], scalar=convp[:, bass.ds(conv + e, 1), k],
                           in1=u_t[:, e], op0=ALU.mult, op1=ALU.add)

            def scaled(pair, e, n):
                read_result(e, n)
                tt(e_pad[:, e, 2:], tmp[:], rstd[:], ALU.mult).then_inc(S("scaled_ready"), 1)

            def up_pair(g, n, pair, c, conv, cols, first=False):
                lo(g, 0, cols)
                if not first:
                    rest_taps(pair - 1, conv - 2)
                lo(g, 1, cols)
                if not first:
                    rest_product(pair - 1)
                scaled(pair, 0, n)
                if not first:
                    rest_lo(pair - 1, c - 1)
                lo(g, 2, cols)
                dve.wait_ge(S("tap_ready"), 2 * pair + 1)
                t = own.mark(taps(conv, 0, 1))
                lo(g, 3, cols)
                own.done(t)
                taps(conv, 0, 0).then_inc(S("gate_ready"), 1)
                scaled(pair, 1, n + 1)

            def rest_taps(pair, conv):
                dve.wait_ge(S("tap_ready"), 2 * pair + 2)
                t = own.mark(taps(conv, 1, 1))
                dve.wait_ge(S("tanh_ready"), pair + 1)
                own.mark(stt(out=u_t[:, 2], in0=u_t[:, 2], scalar=1.0, in1=u_t[:, 0], op0=ALU.add, op1=ALU.mult))
                own.done(t)
                own.value = own.mark(taps(conv, 1, 0))

            def rest_product(pair):
                own.done(own.value)
                stt(out=u_t[:, 3], in0=u_t[:, 2], scalar=0.5, in1=u_t[:, 1], op0=ALU.mult, op1=ALU.mult) \
                    .then_inc(S("product_ready"), 1)

            def rest_lo(pair, c):
                dve.wait_ge(S("feature_hi_ready"), pair + 1)
                tt(chunk(act_in, c, T, 2 * T), u_t[:, 3], chunk(act_in, c).bitcast(F32), ALU.subtract) \
                    .then_inc(S("features_ready"), 1)

            for layer in range(2):
                dve.wait_ge(S("rstd_ready"), 2 + 2 * layer)
                g0, n0, p0 = FIRST_FFN[layer], R_FFN[layer], layer * QUARTERS * G_UP
                for q in range(QUARTERS):
                    final = q == QUARTERS - 1
                    last = G_UP - 1
                    up_pair(g0, n0, p0, 0, 2 * p0, UA, first=True)
                    with own.loop(last, 4, start=1) as i:
                        up_pair(i + g0, 2 * i + n0, i + p0, i, 2 * i + 2 * p0, UA)
                    up_pair(g0 + last, n0 + 2 * last, p0 + last, last, 2 * (p0 + last), UB)
                    rest_taps(p0 + last, 2 * (p0 + last))
                    rest_product(p0 + last)
                    rest_lo(p0 + last, last)
                    g1, n1 = g0 + G_UP, n0 + 2 * G_UP

                    def down_group(i, cols):
                        for s in range(SLOTS):
                            if cols:
                                lo(i + g1, s, cols)
                            add_to_x(4 * i + s, s % 2, 4 * i + (n1 + s),
                                     4 * i + (DC * (1 + 2 * layer) + s + 1) if final else None)

                    with own.loop(G_DOWN - 1, 0 if final else 4) as i:
                        down_group(i, UB)
                    down_group(G_DOWN - 1, None if final and layer == 1 else UA)
                    g0, n0, p0 = g0 + G_QUARTER, n0 + R_QUARTER, p0 + G_UP
                mean_square(2 + 2 * layer)
                if layer == 0:
                    pooling(nc, dve, own, S, x, gain, rstd, win, invc, act_in, split)
                    for i in range(G_POOL):
                        for s in range(SLOTS):
                            lo(FIRST_POOL + i, s, UA)
                            for r in range(2):
                                c = 8 * i + 2 * s + r
                                read_result(r, R_POOL + c)
                                stt(out=x[:, c], in0=tmp[:], scalar=poolp[:, c:c + 1], in1=x[:, c], op0=ALU.mult,
                                    op1=ALU.add).then_inc(x_done, 1)
                                dve.wait_ge(x_done, 2 * DC + c + 1)
                                next_h(3, c, 2 * DC + c + 1)
                    mean_square(3)
            dve.wait_ge(S("rstd_ready"), 5)
            with dve.Fori(0, DC) as c:
                stt(out=chunk(x, c), in0=chunk(x, c), scalar=gain[:, 4, bass.ds(c, 1)], in1=rstd[:], op0=ALU.mult,
                    op1=ALU.mult).then_inc(S("out_ready"), 1)

        @block.tensor
        def _(pe):
            mm = nc.tensor.matmul

            def block_product(bank, s, b, rhs, start, stop):
                cols = slice(b * P, b * P + P)
                mm(acc[bank][:], w_hi[:, s, cols], rhs, start=start, stop=False, skip_group_check=True)
                return mm(acc[bank][:, 0:T], w_lo[:, s, cols], rhs[:, 0:T], start=False, stop=stop,
                          skip_group_check=True)

            def tile(g, e, bank, n, src, ready, count, between=None):
                pe.wait_ge(acc_free, n + 1)
                for half in range(2):
                    s = 2 * e + half
                    pe.wait_ge(lo_ready, 4 * g + (s + 1))
                    pe.wait_ge(ready, count - (8 if half == 0 else 1))
                    for b in range(8):
                        c = 8 * half + b
                        if c == DC - 1:
                            pe.wait_ge(ready, count)
                        ins = block_product(bank, s, b, src[:, c], c == 0, c == DC - 1)
                    ins.then_inc(units_done, 1)
                    if half == 0 and between is not None:
                        square_sum(between)

            def square_sum(n):
                pe.wait_ge(S("summed"), DC * (n + 1))
                mm(aux[:, 4, 0:T], ones[:], ssum[:], start=True, stop=True).then_inc(S("square_sum_ps"), 1)

            pe.wait_ge(params_landed, 16 * N_PARAMS)
            for g in range(G_LOW):
                for e in range(2):
                    tile(g, e, e, 2 * g + e, h, S("h_ready"), DC, 0 if g == e == 0 else None)

            def rwkv(j):
                pe.wait_ge(S("lora_landed"), 16 * j + 16)
                mm(aux[:, 0, 0:T], lora_w[0:LORA, 0], low[0:LORA, 0], start=True, stop=True)
                mm(aux[:, 0, T:2 * T], lora_w[0:LORA, 1], low[0:LORA, 1], start=True, stop=True)
                mm(aux[:, 1, 0:T], lora_w[:, 2], low[:, 2], start=True, stop=False)
                mm(aux[:, 1, 0:T], lora_w[:, 3], low[:, 3], start=False, stop=True).then_inc(S("lora_ps"), 1)
                pe.wait_ge(S("key_squared"), j + 1)
                mm(aux[:, 2, 0:T], mat[:, HEAD_BLOCKS], kn[:], start=True, stop=True).then_inc(S("key_norm_ps"), 1)
                pe.wait_ge(S("bonus_product"), j + 1)
                mm(aux[:, 3, 0:T], mat[:, HEAD_BLOCKS], y_sq[:], start=True, stop=True).then_inc(S("bonus_ps"), 1)
                pe.wait_ge(S("keys_ready"), j + 1)
                for k, src in enumerate((rkv[:, 2, 0:P], rkv[:, 2, P:T], kinv[:, 0], binv[:, 0])):
                    ins = nc.tensor.transpose(aux[:, 4, k * P:k * P + P], src, mat[:, IDENT])
                ins.then_inc(S("turned_ps"), 1)
                pe.wait_ge(S("queries_ready"), j + 1)
                pe.wait_ge(S("bonus_ready"), j + 1)
                for c in range(2):
                    for k, bank in ((kinv, 0), (binv, 2)):
                        for hd in range(2):
                            ch = slice(64 * hd, 64 * hd + 64)
                            ins = mm(aux[:, bank + hd, c * 2 * P:(c + 1) * 2 * P], k[ch, c], kr[ch, c], start=True,
                                     stop=True)
                ins.then_inc(S("grams_ps"), 1)
                pe.wait_ge(S("tok_ready"), j + 1)
                for c in range(2):
                    for hd in range(2):
                        ch = slice(64 * hd, 64 * hd + 64)
                        ins = mm(aux[:, 4 + hd, c * P:c * P + P], kr[ch, c, 0:P], binv[ch, c], start=True, stop=True)
                ins.then_inc(S("grams_ps"), 1)
                for lv in range(LEVELS):
                    pe.wait_ge(S("off_ready"), LEVELS * j + (lv + 1))
                    pe.wait_ge(S("inv_ready"), (LEVELS + 1) * j + (lv + 1))
                    for p in range(4):
                        ins = mm(aux[:, 0, p * P:p * P + P], off[:, p], inv[:, 0, p], start=True, stop=True)
                    ins.then_inc(S("w1_ps"), 1)
                    pe.wait_ge(S("w1_ready"), LEVELS * j + (lv + 1))
                    for p in range(4):
                        ins = mm(aux[:, 2, p * P:p * P + P], inv[:, 1, p], w1[:, p], start=True, stop=True)
                    if lv < LEVELS - 1:
                        for p in range(4):
                            ins = mm(aux[:, 3, p * P:p * P + P], w1[:, p], inv[:, 1, p], start=True, stop=True)
                    ins.then_inc(S("inv_ps"), 1)
                pe.wait_ge(S("inv_ready"), (LEVELS + 1) * j + (LEVELS + 1))
                for c in range(2):
                    if c:
                        pe.wait_ge(S("state_ready"), j + 1)
                        mm(aux[:, 1, 0:P], kr[:, 1, 0:P], state[:], start=True, stop=False, skip_group_check=True)
                    for hd in range(2):
                        v = slice(64 * hd, 64 * hd + 64)
                        ins = mm(aux[:, 1, v], akr[:, 2 * hd + c, 0:P], tok[:, c, v], start=c == 0, stop=True,
                                 skip_group_check=True)
                    ins.then_inc(S("ru_ps"), 1)
                    pe.wait_ge(S("ru_ready"), 4 * j + (2 * c + 1))
                    for hd in range(2):
                        v = slice(64 * hd, 64 * hd + 64)
                        ins = mm(aux[:, 1, v], inv[:, 0, 2 * hd + c], ru[:, 0, v], start=True, stop=True)
                    ins.then_inc(S("ru_ps"), 1)
                    pe.wait_ge(S("ru_ready"), 4 * j + (2 * c + 2))
                    if c == 0:
                        mm(aux[:, 4, 0:P], tok[:, 2], tok[:, 0], start=True, stop=False)
                        mm(aux[:, 4, 0:P], tok[:, 3], ru[:, 1], start=False, stop=True).then_inc(S("state_ps"), 1)
                    else:
                        mm(aux[:, 5, P:T], state[:], kr[:, 1, P:2 * P], start=True, stop=False,
                           skip_group_check=True)
                    for hd in range(2):
                        v = slice(64 * hd, 64 * hd + 64)
                        dst = aux[v, 5, c * P:c * P + P]
                        mm(dst, tok[:, c, v], akr[:, 2 * hd + c, P:2 * P], start=c == 0, stop=False,
                           skip_group_check=True)
                        ins = mm(dst, ru[:, 1, v], abr[:, 2 * hd + c, P:2 * P], start=False, stop=True,
                                 skip_group_check=True)
                ins.then_inc(S("y_ps"), 1)
                pe.wait_ge(S("y_ready"), j + 1)
                mm(aux[:, 2, 0:T], mat[:, HEAD_BLOCKS], y[:], start=True, stop=True).then_inc(S("mean_ps"), 1)
                pe.wait_ge(S("y_squared"), j + 1)
                mm(aux[:, 3, 0:T], mat[:, HEAD_BLOCKS], y_sq[:], start=True, stop=True).then_inc(S("var_ps"), 1)

            pe.wait_ge(S("low_ready"), 1)
            with pe.Fori(0, PAIRS) as j:
                for e in range(2):
                    for t in range(2):
                        tile(2 * j + (FIRST_RW + e), t, t, 4 * j + (2 * FIRST_RW + 2 * e + t), h, S("h_ready"), DC)
                rwkv(j)

            def fox(n):
                pe.wait_ge(S("qv_ready"), n + 1)
                q, v = qv[:, 0], qv[:, 1]
                k, row = fox_k[:, bass.ds(n, 1)], forget_row[0:1, bass.ds(n * T, T)]
                kf = k.rearrange("p o t -> p (o t)")
                k_first = fox_k[:, bass.ds(n, 1), 0:P].rearrange("p o t -> p (o t)")
                mm(aux[:, 0, 0:P], q[:, 0:P], k_first, start=True, stop=False)
                mm(aux[:, 0, 0:P], ones[0:1, :], forget_row[0:1, bass.ds(n * T, P)], start=False, stop=True)
                mm(aux[:, 0, P:3 * P], q[:, P:T], kf, start=True, stop=False)
                mm(aux[:, 0, P:3 * P], ones[0:1, :], row, start=False, stop=True).then_inc(S("scores_ps"), 1)
                pe.wait_ge(S("probs_ready"), n + 1)
                for b in range(3):
                    nc.tensor.transpose(aux[:, 1, b * P:b * P + P], prob[:, b * P:b * P + P], mat[:, IDENT])
                for b in range(2):
                    ins = nc.tensor.transpose(aux[:, 2, b * P:b * P + P], v[:, b * P:b * P + P], mat[:, IDENT])
                ins.then_inc(S("fox_turned_ps"), 1)
                pe.wait_ge(S("fox_turned"), n + 1)
                mm(aux[:, 3, 0:P], v_tok[:, 0], prob_t[:, 0:P], start=True, stop=True)
                mm(aux[:, 3, P:T], v_tok[:, 0], prob_t[:, P:2 * P], start=True, stop=False)
                mm(aux[:, 3, P:T], v_tok[:, 1], prob_t[:, 2 * P:3 * P], start=False, stop=True) \
                    .then_inc(S("attn_ps"), 1)

            pe.wait_ge(S("forget_row_landed"), 16)
            with pe.Fori(0, HEADS) as n:
                for t in range(2):
                    tile(n + FIRST_FOX, t, t, 2 * n + (2 * FIRST_FOX + t), h, S("h_ready"), DC)
                fox(n)

            with pe.Fori(0, G_OUT) as i:
                for e in range(2):
                    tile(i + FIRST_OUT, e, e, 2 * i + (2 * FIRST_OUT + e), act_in, S("mixed_ready"), DC)

            for layer in range(2):
                g0, n0, f0 = FIRST_FFN[layer], R_FFN[layer], layer * QUARTERS * G_UP
                for q in range(QUARTERS):
                    def up(i, between=None):
                        for e in range(2):
                            tile(i + g0, e, e, 2 * i + (n0 + e), h, S("h_ready"), DC * (layer + 2),
                                 between if e == 0 else None)
                    if q == 0:
                        up(0, 1 + 2 * layer)
                        with pe.Fori(1, G_UP) as i:
                            up(i)
                    else:
                        with pe.Fori(0, G_UP) as i:
                            up(i)
                    with pe.Fori(0, G_DOWN) as i:
                        for s in range(SLOTS):
                            pe.wait_ge(acc_free, 4 * i + (n0 + 2 * G_UP + s + 1))
                            pe.wait_ge(lo_ready, 4 * i + (4 * (g0 + G_UP) + s + 1))
                            pe.wait_ge(S("features_ready"), f0 + G_UP - 1)
                            for b in range(FC):
                                if b == FC - 1:
                                    pe.wait_ge(S("features_ready"), f0 + G_UP)
                                ins = block_product(s % 2, s, b, act_in[:, b], b == 0, b == FC - 1)
                            ins.then_inc(units_done, 1)
                    g0, n0, f0 = g0 + G_QUARTER, n0 + R_QUARTER, f0 + G_UP
                square_sum(2 + 2 * layer)
                if layer == 0:
                    for i in range(G_POOL):
                        for s in range(SLOTS):
                            u = 4 * i + s
                            pe.wait_ge(lo_ready, 4 * (FIRST_POOL + i) + s + 1)
                            pe.wait_ge(S("pooled_ready"), 4 * (u // 2) + 4)
                            for r in range(2):
                                pe.wait_ge(acc_free, R_POOL + 2 * u + r + 1)
                                for b in range(4):
                                    ins = block_product(r, s, 4 * r + b, act_in[:, 4 * (u // 2) + b], b == 0, b == 3)
                            ins.then_inc(units_done, 1)


N_CONSTS, N_PARAMS = 6, 7


def pooling(nc, dve, own, S, x, gain, rstd, win, invc, act_in, split):
    tt, stt = nc.vector.tensor_tensor, nc.vector.scalar_tensor_tensor
    nc.vector.memset(win[:, :, 0:16], 0.0).then_inc(S("win_cleared"), 1)
    dve.wait_ge(S("win_cleared"), 1)
    dve.wait_ge(S("counts_landed"), 16)
    dve.wait_ge(S("rstd_ready"), 3)
    for g in range(len((2, 4, 8, 16))):
        with own.loop(4, 5 + g) as i:
            c = i + 4 * g
            own.link(stt(out=win[:, 0, 16:], in0=chunk(x, c), scalar=gain[:, 1, bass.ds(c, 1)], in1=rstd[:],
                         op0=ALU.mult, op1=ALU.mult))
            src = 0
            for k in range(g + 1):
                dst = 1 + k % 2
                own.link(tt(win[:, dst, 16:], win[:, src, 16:], win[:, src, 16 - 2 ** k:16 - 2 ** k + T], ALU.add))
                src = dst
            own.link(tt(win[:, src, 16:], win[:, src, 16:], invc[:, g], ALU.mult))
            own.link(tt(win[:, src, 16:], win[:, src, 16:], win[:, 0, 16:], ALU.subtract))
            split(act_in, c, win[:, src, 16:]).then_inc(S("pooled_ready"), 1)


def _tables():
    import numpy as np
    row, col = np.arange(P)[:, None], np.arange(P)[None, :]
    low = lambda b: (row // (2 * b) == col // (2 * b)) & (row // b % 2 == 1) & (col // b % 2 == 0)
    mats = [low(2 ** (lv + 1)) for lv in range(LEVELS)] + [low(1), low(1).T, row == col, row // 64 == col // 64]
    mats += [np.where(row >= col, 0, -1e30), row < col, row <= col, row > col]
    mats = np.stack([m.astype(np.float32) for m in mats], 1)
    t = np.arange(T)
    count = np.stack([(1 / np.minimum(t + 1, w)).astype(np.float32) for w in (2, 4, 8, 16)])
    return mats, np.broadcast_to(count, (P, 4, T)).copy()


def _layouts(a):
    import numpy as np
    f = {k: np.asarray(v) for k, v in a.items()}
    cols = lambda v: np.ascontiguousarray(v.reshape(-1, P).T)

    def halves(w):
        m = w.shape[1] // P
        return w.reshape(2, 8, P, m, P).transpose(3, 0, 2, 1, 4).reshape(2 * m, P, UA)

    def pad(v, n=P):
        return np.concatenate([v, np.zeros(v.shape[:-1] + (n - v.shape[-1],), v.dtype)], -1)

    W = HEADS * P
    fox, rw = 3 * W + HEADS, 3 * W
    w_in, mu = f["w_in"][0], f["shift_mu"][0]
    wd, ad, gd = fox + rw, fox + rw + LORA, fox + rw + 2 * LORA
    order = [pad(np.concatenate([w_in[:, ad:ad + LORA], w_in[:, 3 * W:fox]], 1)), pad(w_in[:, wd:wd + LORA]),
             w_in[:, gd:]]
    for j in range(PAIRS):
        order.append(w_in[:, W + j * P:W + j * P + P])
        order += [w_in[:, fox + k * W + j * P:fox + k * W + j * P + P] for k in range(3)]
    for n in range(HEADS):
        order += [w_in[:, k * W + n * P:k * W + n * P + P] for k in (0, 2)]
    w_out = np.concatenate([f["w_out"][0][W:], f["w_out"][0][:W]], 0)
    pool = f["w_pool"][0].reshape(4, 4, P, 2, 2, P).transpose(0, 3, 2, 4, 1, 5).reshape(8, P, UA)
    ups = [halves(w.reshape(D, 2, D_FF // P, P).transpose(0, 2, 1, 3).reshape(D, 2 * D_FF)) for w in f["w_ffn_up"]]
    wa = np.concatenate([halves(np.concatenate(order, 1)), halves(w_out), ups[0], pool, ups[1]], 0)
    wb = np.concatenate([w.reshape(QUARTERS, FC, P, DC, P).transpose(0, 3, 2, 1, 4).reshape(QUARTERS * DC, P, UB)
                         for w in f["w_ffn_down"]], 0)
    mix = np.stack([cols(v) for v in (mu[0:W], mu[W:2 * W], mu[2 * W:3 * W], f["w0"][0], f["a0"][0], f["k_k"][0],
                                      f["k_a"][0], f["r_k"][0].reshape(-1), f["gn_w"][0], f["gn_b"][0])], 2)
    wd, ad, gd = rw, rw + LORA, rw + 2 * LORA
    mu0 = np.stack([pad(mu[ad:ad + LORA]), pad(mu[wd:wd + LORA]), mu[gd:gd + P], mu[gd + P:gd + 2 * P]], 1)
    b_f = np.zeros((P, 1), np.float32)
    b_f[LORA:LORA + HEADS, 0] = f["b_f"][0]
    rows = lambda w: pad(w.T).T.reshape(P, PAIRS, P).transpose(1, 0, 2)
    gate = f["w_gate_up"][0].reshape(2, P, PAIRS, P).transpose(2, 1, 0, 3)
    lora = np.concatenate([rows(f["w_iclr_up"][0])[:, :, None], rows(f["w_decay_up"][0])[:, :, None], gate], 2)
    lora = np.concatenate([lora, np.zeros((1,) + lora.shape[1:], lora.dtype)], 0)
    conv = np.concatenate([f["conv_w"], f["conv_b"][:, None]], 1)
    conv = conv.reshape(2, 4, 2, D_FF // P, P).transpose(4, 0, 3, 2, 1).reshape(P, -1, 4)
    gains = np.stack([cols(v) for v in (f["mix_norm"][0], f["pool_norm"][0], f["ffn_norm"][0], f["ffn_norm"][1],
                                        f["final_norm"])], 1)
    x = f["x"][0].T.reshape(DC, P, T).transpose(1, 0, 2)
    mats, count = _tables()
    named = dict(x_in=x, gains=gains, wa=wa, wb=wb, mix_p=mix, mu0=mu0, b_f=b_f, lora=lora, conv_p=conv,
                 pool_p=cols(f["pool_scale"][0]), mats=mats, inv_count=count)
    return {k: np.ascontiguousarray(v) for k, v in named.items()}


def kernel(**inputs):
    import concourse.bacc as _bacc
    from concourse.bass_utils import run_bass_kernel_spmd as _run

    nc = _bacc.Bacc("TRN2", target_bir_lowering=False, num_devices=1)
    arrays = _layouts(inputs)
    args = {k: nc.dram_tensor(f"{k}_dram", v.shape, mybir.dt.from_np(v.dtype), kind="ExternalInput").ap()
            for k, v in arrays.items()}
    out = nc.dram_tensor("out_dram", (P, DC, T), F32, kind="ExternalOutput").ap()
    trunk(nc, out=out, **args)
    r = _run(nc, [{f"{k}_dram": v for k, v in arrays.items()}], core_ids=[0])
    return r.results[0]["out_dram"].transpose(2, 1, 0).reshape(1, T, D)
```

```python
from contextlib import ExitStack, contextmanager

import concourse.bass as bass
from concourse import mybir

F32 = mybir.dt.float32
F32R = mybir.dt.float32r
U8 = mybir.dt.uint8
ALU = mybir.AluOpType
ACT = mybir.ActivationFunctionType
AX = mybir.AxisListType

P = 128
T = 256
D = 2048
DC = D // P
HEADS = 8
PAIRS = 8
LORA = 96
D_FF = 5632
QUARTERS = 4
FC = D_FF // P // QUARTERS
RMS_EPS = 1e-6
GN_EPS = 64e-5
EXP_HALF = 0.6065306597126334
ATT_SCALE = P ** -0.5
SLOTS = 4
UA = 8 * P
UB = FC * P
LEVELS = 6

MU_R, MU_K, MU_V, W0, A0, K_K, K_A, R_K, GN_W, GN_B = range(10)
ONE_LOW, ONE_UP, IDENT, HEAD_BLOCKS, CAUSAL, MASKS = 6, 7, 8, 9, 10, 11
TILES = 6
G_LOW, G_IN, G_OUT = 2, PAIRS * TILES // 2, DC // 2
G_UP, G_DOWN, G_POOL = FC, DC // SLOTS, 2
G_QUARTER = G_UP + G_DOWN
FIRST_IN = G_LOW
FIRST_OUT = FIRST_IN + G_IN
FIRST_FFN0 = FIRST_OUT + G_OUT
FIRST_POOL = FIRST_FFN0 + QUARTERS * G_QUARTER
FIRST_FFN1 = FIRST_POOL + G_POOL
FIRST_FFN = (FIRST_FFN0, FIRST_FFN1)
R_QUARTER = 2 * G_UP + 4 * G_DOWN
R_POOL = 2 * FIRST_FFN0 + QUARTERS * R_QUARTER
R_FFN = (2 * FIRST_FFN0, R_POOL + DC)


class Chain:

    def __init__(self, eng, sem):
        self.eng, self.sem, self.base, self.k = eng, sem, 0, 0

    def link(self, ins):
        self.k += 1
        ins.then_inc(self.sem, 1)
        self.eng.wait_ge(self.sem, self.base + self.k)

    def mark(self, ins):
        self.k += 1
        ins.then_inc(self.sem, 1)
        return self.base + self.k

    def done(self, count):
        self.eng.wait_ge(self.sem, count)

    @contextmanager
    def loop(self, count, per, start=0):
        base = self.base + self.k
        with self.eng.Fori(start, count) as i:
            self.base, self.k = per * i + (base - per * start), 0
            yield i
            assert self.k == per, (self.k, per)
        self.base, self.k = base + per * (count - start), 0


def chunk(t, c, lo=0, hi=T):
    return t[:, bass.ds(c, 1), lo:hi].rearrange("p o t -> p (o t)")


def trunk(nc, x_in, gains, wa, wb, mix_p, mu0, b_f, lora, conv_p, pool_p, mats, inv_count, out):
    with ExitStack() as ctx:
        def sb(name, shape, dt=F32):
            return ctx.enter_context(nc.sbuf_tensor(name, shape, dt))

        def sem(name):
            return ctx.enter_context(nc.semaphore(name))

        x = sb("x", [P, DC, T])
        h = sb("h", [P, DC, 2 * T], F32R)
        w_raw = sb("w_raw", [P, SLOTS, UB])
        w_hi = sb("w_hi", [P, SLOTS, UB], F32R)
        w_lo = sb("w_lo", [P, SLOTS, UB], F32R)
        gain = sb("gain", [P, 5, DC])
        mixp = sb("mixp", [P, PAIRS, 10])
        mu_low = sb("mu_low", [P, 4])
        bf = sb("bf", [P, 1])
        convp = sb("convp", [P, 2 * 2 * FC * QUARTERS, 4])
        poolp = sb("poolp", [P, DC])
        mask = sb("mask", [P, 2, 3 * P], U8)
        mat = sb("mat", [P, 14, P])
        ones = sb("ones", [P, P])
        sq = sb("sq", [P, T])
        ssum = sb("ssum", [P, T])
        ms = sb("ms", [P, T])
        rstd = sb("rstd", [P, T])
        tmp = sb("tmp", [P, T])
        cross = sb("cross", [P, 2, T])
        e_pad = sb("e_pad", [P, 2, 2 + T])
        forget = sb("forget", [P, 2, T])
        mixed = sb("mixed", [P, PAIRS + HEADS, T])

        prob = w_raw[:, 0, UA:UA + 3 * P]
        prob_t = w_raw[:, 1, UA:UA + 3 * P]
        v_tok = w_raw[:, 2, UA:UA + 2 * P]
        row_stats = w_raw[:, 3, UA:UA + 4]
        row_max, row_sum = row_stats[:, 0:2], row_stats[:, 2:4]

        scope = ExitStack()

        def shared(name, shape, dt=F32):
            return scope.enter_context(nc.sbuf_tensor(name, shape, dt))

        low = shared("low", [P, 4, T])
        lora_w = shared("lora_w", [P, 2, P])
        gate_w = shared("gate_w", [P, 2, P])
        qkv = shared("qkv", [P, 3, T])
        forget_sel = shared("forget_sel", [P, T])
        rkv = shared("rkv", [P, 3, T])
        gate = shared("gate", [P, T])
        iclr = shared("iclr", [P, T])
        log_w = shared("log_w", [P, T])
        kk = shared("kk", [P, T])
        kn = shared("kn", [P, T])
        rs = shared("rs", [P, T])
        cum = shared("cum", [P, 2, P + 1])
        neg_mid = shared("neg_mid", [P, 2])
        dec = shared("dec", [P, 2, P + 1])
        inv_dec = shared("inv_dec", [P, 2, P + 1])
        kr = shared("kr", [P, 2, 2 * P])
        kinv = shared("kinv", [P, 2, P])
        binv = shared("binv", [P, 2, P])
        tok = shared("tok", [P, 4, P])
        akr = shared("akr", [P, 4, 2 * P])
        abr = shared("abr", [P, 4, 2 * P])
        al = shared("al", [P, 4, P])
        inv = shared("inv", [P, 2, 4, P])
        off = shared("off", [P, 4, P])
        w1 = shared("w1", [P, 4, P])
        ru = shared("ru", [P, 2, P])
        state = shared("state", [P, P])
        state_scale = shared("state_scale", [P, 1])
        y = shared("y", [P, T])
        y_sq = shared("y_sq", [P, T])
        var = shared("var", [P, T])
        scope.close()
        act_in = sb("act_in", [P, DC, 2 * T], F32R)
        scope.close()
        u_t = sb("u_t", [P, 4, T])
        invc = sb("invc", [P, 4, T])
        win = sb("win", [P, 3, 16 + T])

        acc = [ctx.enter_context(nc.psum_tensor(f"acc{b}", [P, 512], F32)) for b in range(2)]
        aux = ctx.enter_context(nc.psum_tensor("aux", [P, 6, 512], F32))

        params_landed = sem("params_landed")
        x_landed = sem("x_landed")
        w_landed = [sem(f"w_landed{s}") for s in range(SLOTS)]
        names = {}

        def S(name):
            if name not in names:
                names[name] = sem(name)
            return names[name]

        hi_ready, lo_ready, units_done = S("hi_ready"), S("lo_ready"), S("units_done")
        acc_free = S("acc_free")
        x_done = S("x_chunks_final")

        def mat_b(k, n):
            return mat[:, k:k + 1, :].to_broadcast([P, n, P])

        block = ctx.enter_context(nc.Block())

        @block.sync
        def _(sp):
            sp.dma_start(x[:], x_in).then_inc(x_landed, 16)
            sp.dma_start(gain[:], gains).then_inc(params_landed, 16)
            for s in range(SLOTS):
                sp.dma_start(w_raw[:, s, 0:UA], wa[s]).then_inc(w_landed[s], 16)
            for dst, src in ((mixp, mix_p), (mu_low, mu0), (bf, b_f), (mat, mats), (convp, conv_p),
                             (poolp, pool_p)):
                sp.dma_start(dst[:], src).then_inc(params_landed, 16)

            def load(w, first, g, n, cols):
                with sp.Fori(0, n) as i:
                    for s in range(SLOTS):
                        sp.wait_ge(lo_ready, 4 * i + (4 * g + s - 3))
                        src = w[bass.ds(4 * i + (4 * first + s), 1)].rearrange("o p c -> (o p) c")
                        sp.dma_start(w_raw[:, s, 0:cols], src).then_inc(w_landed[s], 16)

            load(wa, 1, 1, FIRST_FFN0 - 1, UA)
            sp.wait_ge(S("mixed_ready"), PAIRS + HEADS)
            sp.dma_start(invc[:], inv_count).then_inc(S("counts_landed"), 16)
            g, a, b = FIRST_FFN0, FIRST_FFN0, 0
            for layer in range(2):
                for q in range(QUARTERS):
                    load(wa, a, g, G_UP, UA)
                    load(wb, b, g + G_UP, G_DOWN, UB)
                    g, a, b = g + G_QUARTER, a + G_UP, b + G_DOWN
                if layer == 0:
                    load(wa, a, g, G_POOL, UA)
                    g, a = g + G_POOL, a + G_POOL
            sp.wait_ge(S("out_ready"), DC)
            sp.dma_start(out, x[:]).then_inc(S("out_stored"), 16)
            sp.wait_ge(S("out_stored"), 16)

        @block.gpsimd
        def _(pool):
            consts = S("consts_ready")
            for t, v in ((ones, 1.0), (e_pad, 0.0), (cum, 0.0), (akr, 0.0),
                         (abr, 0.0), (al, 0.0), (forget_sel, 0.0)):
                nc.gpsimd.memset(t[:], v).then_inc(consts, 1)
            pool.wait_ge(consts, N_CONSTS)

            def norm(n):
                if n == 0:
                    pool.wait_ge(x_landed, 16)
                else:
                    pool.wait_ge(S("mean_square_ready"), n)
                nc.gpsimd.memset(ssum[:], 0.0).then_inc(S("sum_cleared"), 1)
                pool.wait_ge(S("sum_cleared"), n + 1)
                with pool.Fori(0, DC) as c:
                    if n:
                        pool.wait_ge(x_done, c + (DC * (n - 1) + 1))
                    nc.gpsimd.tensor_tensor(sq[:], chunk(x, c), chunk(x, c), ALU.mult).then_inc(S("squared"), 1)
                    pool.wait_ge(S("squared"), c + (DC * n + 1))
                    nc.gpsimd.tensor_tensor(ssum[:], ssum[:], sq[:], ALU.add).then_inc(S("summed"), 1)
                    pool.wait_ge(S("summed"), c + (DC * n + 1))

            norm(0)
            with pool.Fori(0, PAIRS) as j:
                pool.wait_ge(S("al_masked"), 2 * j + 2)
                for lv in range(LEVELS):
                    if lv:
                        pool.wait_ge(S("w1_ps"), LEVELS * j + lv)
                    nc.gpsimd.tensor_tensor(off[:], al[:], mat_b(lv, 4), ALU.mult).then_inc(S("off_ready"), 1)
            for n in range(1, 5):
                norm(n)

        @block.scalar
        def _(act):
            def hi(g, s, cols):
                act.wait_ge(w_landed[s], 16 * g + 32)
                act.wait_ge(units_done, 4 * g + (s + 1))
                nc.scalar.activation(w_hi[:, s, 0:cols], w_raw[:, s, 0:cols], ACT.Identity).then_inc(hi_ready, 1)

            def cross_half(bank, done):
                act.wait_ge(units_done, done)
                nc.scalar.activation(cross[:, bank], acc[bank][:, T:2 * T], ACT.Identity).then_inc(S("cross_ready"), 1)

            def tile(g, e, cols):
                hi(g, 2 * e, cols)
                cross_half(e, 4 * g + (2 * e + 2))
                hi(g, 2 * e + 1, cols)

            def root(n):
                act.wait_ge(S("mean_square_ready"), n + 1)
                nc.scalar.activation(ms[:], ms[:], ACT.Sqrt).then_inc(S("rms_ready"), 1)

            def next_h(which, c, n):
                act.wait_ge(x_done, n)
                nc.scalar.activation(chunk(h, c), chunk(x, c), ACT.Identity,
                                     scale=gain[:, which, bass.ds(c, 1)]).then_inc(S("h_hi_ready"), 1)

            act.dma_start(lora_w[:], lora[0, :, 0:2]).then_inc(S("lora_landed"), 16)
            act.dma_start(gate_w[:], lora[0, :, 2:4]).then_inc(S("gate_landed"), 16)
            act.wait_ge(x_landed, 16)
            act.wait_ge(params_landed, 16 * N_PARAMS)
            for s in range(SLOTS):
                act.wait_ge(w_landed[s], 16)
                nc.scalar.activation(w_hi[:, s, 0:UA], w_raw[:, s, 0:UA], ACT.Identity).then_inc(hi_ready, 1)
            with act.Fori(0, DC) as c:
                nc.scalar.activation(chunk(h, c), chunk(x, c), ACT.Identity,
                                     scale=gain[:, 0, bass.ds(c, 1)]).then_inc(S("h_hi_ready"), 1)
            root(0)
            for g in range(G_LOW):
                for e in range(2):
                    tile(g, e, UA)
            act.wait_ge(S("low_shifted"), 1)
            nc.scalar.activation(low[0:LORA, 1], low[0:LORA, 1], ACT.Tanh).then_inc(S("low_tanh"), 1)
            nc.scalar.activation(low[:, 2:4], low[:, 2:4], ACT.Tanh, scale=0.5).then_inc(S("low_tanh"), 1)
            act.wait_ge(S("forget_abs"), 1)
            fg = forget[LORA:LORA + HEADS, 1]
            nc.scalar.activation(fg, fg, ACT.Exp, scale=-1.0).then_inc(S("forget_exp"), 1)
            act.wait_ge(S("forget_exp"), 1)
            nc.scalar.activation(fg, fg, ACT.Ln, bias=ones[LORA:LORA + HEADS, 0:1]).then_inc(S("forget_ln"), 1)

            def unit_hi(i, u):
                hi(TILES // 2 * i + (FIRST_IN + u // SLOTS), u % SLOTS, UA)

            def cross_of(i, t):
                cross_half(t % 2, 2 * TILES * i + (SLOTS * FIRST_IN + 2 * t + 2))

            def low_rank(i):
                par = lambda k: mixp[:, bass.ds(i, 1), k]
                act.wait_ge(S("lora_ps"), i + 1)
                act.dma_start(lora_w[:], lora[bass.ds(i + 1, 1), :, 0:2].rearrange("o p a b -> (o p) a b")) \
                    .then_inc(S("lora_landed"), 16)
                nc.scalar.activation(iclr[:], aux[:, 4, 0:T], ACT.Tanh, scale=0.5, bias=par(A0))
                nc.scalar.activation(log_w[:], aux[:, 4, T:2 * T], ACT.Tanh, scale=0.5, bias=par(W0)) \
                    .then_inc(S("lora_read"), 1)

            def decays(i):
                act.wait_ge(S("cum_ready"), i + 1)
                for c in range(2):
                    nc.scalar.activation(dec[:, c], cum[:, c], ACT.Exp, bias=neg_mid[:, c:c + 1])
                for c in range(2):
                    ins = nc.scalar.activation(inv_dec[:, c], cum[:, c], ACT.Exp, scale=-1.0,
                                               bias=cum[:, c, P // 2:P // 2 + 1])
                ins.then_inc(S("decay_ready"), 1)

            def copy_w1(j, lv):
                act.wait_ge(S("w1_ps"), LEVELS * j + (lv + 1))
                nc.scalar.activation(w1[:], aux[:, 0].rearrange("p (a b) -> p a b", a=4), ACT.Identity) \
                    .then_inc(S("w1_ready"), 1)

            def copy_ru(j, k):
                act.wait_ge(S("ru_ps"), 4 * j + (k + 1))
                nc.scalar.activation(ru[:, k % 2], aux[:, 0, 0:P], ACT.Identity).then_inc(S("ru_ready"), 1)

            def body(i, mix, load):
                j = i - 1
                par = lambda k: mixp[:, bass.ds(j, 1), k]
                if load:
                    unit_hi(i, 0)
                    cross_of(i, 0)
                    unit_hi(i, 1)
                if mix:
                    copy_w1(j, 0)
                if load:
                    unit_hi(i, 2)
                if mix:
                    copy_w1(j, 1)
                if load:
                    cross_of(i, 1)
                    unit_hi(i, 3)
                if mix:
                    act.wait_ge(S("scores_ready"), j + 1)
                    nc.scalar.activation(prob[:, 0:P], prob[:, 0:P], ACT.Exp, scale=ATT_SCALE, bias=row_max[:, 0:1],
                                         accum_out=row_sum[:, 0:1])
                    nc.scalar.activation(prob[:, P:3 * P], prob[:, P:3 * P], ACT.Exp, scale=ATT_SCALE,
                                         bias=row_max[:, 1:2], accum_out=row_sum[:, 1:2]).then_inc(S("exp_ready"), 1)
                    copy_w1(j, 2)
                if load:
                    unit_hi(i, 4)
                if mix:
                    act.wait_ge(S("fox_turned_ps"), j + 1)
                    nc.scalar.activation(prob_t, aux[:, 4, 0:3 * P], ACT.Identity)
                    nc.scalar.activation(v_tok, aux[:, 5, 0:T], ACT.Identity).then_inc(S("fox_turned"), 1)
                    copy_w1(j, 3)
                if load:
                    cross_of(i, 2)
                    unit_hi(i, 5)
                if mix:
                    copy_w1(j, 4)
                if load:
                    low_rank(i)
                    unit_hi(i, 6)
                if mix:
                    copy_w1(j, 5)
                    copy_ru(j, 0)
                if load:
                    decays(i)
                    cross_of(i, 3)
                if mix:
                    copy_ru(j, 1)
                if load:
                    unit_hi(i, 7)
                    act.wait_ge(S("key_norm_ready"), i + 1)
                    nc.scalar.activation(rs[:], rs[:], ACT.Sqrt).then_inc(S("key_root_ready"), 1)
                    unit_hi(i, 8)
                if mix:
                    copy_ru(j, 2)
                if load:
                    cross_of(i, 4)
                if mix:
                    copy_ru(j, 3)
                if load:
                    unit_hi(i, 9)
                if mix:
                    act.wait_ge(S("y_ps"), j + 1)
                    nc.scalar.activation(y[:], aux[:, 3, 0:T], ACT.Identity).then_inc(S("y_ready"), 1)
                    act.wait_ge(S("gate_ps"), j + 1)
                    act.dma_start(gate_w[:], lora[bass.ds(j + 1, 1), :, 2:4].rearrange("o p a b -> (o p) a b")) \
                        .then_inc(S("gate_landed"), 16)
                    nc.scalar.activation(gate[:], aux[:, 3, 0:T], ACT.Identity).then_inc(S("gate_read"), 1)
                    act.wait_ge(S("y_centred"), j + 1)
                    nc.scalar.activation(y_sq[:], y[:], ACT.Square).then_inc(S("y_squared"), 1)
                if load:
                    unit_hi(i, 10)
                    act.wait_ge(S("turned_ps"), i + 1)
                    nc.scalar.activation(tok[:], aux[:, 4].rearrange("p (a b) -> p a b", a=4), ACT.Identity) \
                        .then_inc(S("tok_ready"), 1)
                if mix:
                    act.wait_ge(S("var_ready"), j + 1)
                    nc.scalar.activation(var[:], var[:], ACT.Sqrt).then_inc(S("group_root_ready"), 1)
                if load:
                    cross_of(i, 5)
                    unit_hi(i, 11)
                if mix:
                    act.wait_ge(S("y_scaled"), j + 1)
                    nc.scalar.activation(y[:], y[:], ACT.Identity, scale=par(GN_W), bias=par(GN_B)) \
                        .then_inc(S("group_norm_ready"), 1)

            act.wait_ge(S("halved"), 1)
            body(0, False, True)
            with act.Fori(1, PAIRS) as i:
                body(i, True, True)
            body(PAIRS, True, False)

            act.wait_ge(S("rwkv_done"), PAIRS)
            act.wait_ge(S("attn_done"), HEADS)
            act.wait_ge(S("lora_landed"), 16 * (PAIRS + 1))
            act.wait_ge(S("gate_landed"), 16 * (PAIRS + 1))
            with act.Fori(0, PAIRS + HEADS) as c:
                nc.scalar.activation(chunk(act_in, c), chunk(mixed, c), ACT.Identity).then_inc(S("mixed_hi_ready"), 1)

            def out_group(i, cols=UA):
                for e in range(2):
                    tile(i + FIRST_OUT, e, cols)
                    next_h(2, 2 * i + e, 2 * i + (e + 1))

            with act.Fori(0, G_OUT) as i:
                out_group(i)

            def feature_hi(pair, c):
                act.wait_ge(S("product_ready"), pair + 1)
                nc.scalar.activation(chunk(act_in, c), u_t[:, 3], ACT.Identity).then_inc(S("feature_hi_ready"), 1)

            def tap(pair, conv, e):
                act.wait_ge(S("scaled_ready"), 2 * pair + (e + 1))
                par = lambda k: convp[:, bass.ds(conv + e, 1), k]
                nc.scalar.activation(u_t[:, e], e_pad[:, e, 2:], ACT.Identity, scale=par(2), bias=par(3)) \
                    .then_inc(S("tap_ready"), 1)

            def up_pair(g, pair, c, conv, cols, first=False):
                hi(g, 0, cols)
                cross_half(0, 4 * g + 2)
                if not first:
                    feature_hi(pair - 1, c - 1)
                hi(g, 1, cols)
                tap(pair, conv, 0)
                hi(g, 2, cols)
                act.wait_ge(S("gate_ready"), pair + 1)
                nc.scalar.activation(u_t[:, 2], u_t[:, 0], ACT.Tanh, scale=0.5).then_inc(S("tanh_ready"), 1)
                cross_half(1, 4 * g + 4)
                hi(g, 3, cols)
                tap(pair, conv, 1)

            for layer in range(2):
                g0, p0 = FIRST_FFN[layer], layer * QUARTERS * G_UP
                for q in range(QUARTERS):
                    if q == 0:
                        root(1 + 2 * layer)
                    up_pair(g0, p0, 0, 2 * p0, UA, first=True)
                    with act.Fori(1, G_UP - 1) as i:
                        up_pair(i + g0, i + p0, i, 2 * i + 2 * p0, UA)
                    last = G_UP - 1
                    up_pair(g0 + last, p0 + last, last, 2 * (p0 + last), UB)
                    feature_hi(p0 + last, last)
                    with act.Fori(0, G_DOWN - 1) as i:
                        for s in range(SLOTS):
                            hi(i + (g0 + G_UP), s, UB)
                            cross_half(s % 2, 4 * i + (4 * (g0 + G_UP) + s + 1))
                    for s in range(SLOTS):
                        if not (layer == 1 and q == QUARTERS - 1):
                            hi(g0 + G_QUARTER - 1, s, UA)
                        cross_half(s % 2, 4 * (g0 + G_QUARTER - 1) + s + 1)
                    g0, p0 = g0 + G_QUARTER, p0 + G_UP
                if layer == 0:
                    root(2)
                    for i in range(G_POOL):
                        for s in range(SLOTS):
                            hi(FIRST_POOL + i, s, UA)
                            for r in range(2):
                                cross_half(r, 4 * (FIRST_POOL + i) + s + 1)
                            for r in range(2):
                                c = 8 * i + 2 * s + r
                                next_h(3, c, 2 * DC + c + 1)
            root(4)

        @block.vector
        def _(dve):
            own = Chain(dve, S("dve_own"))
            tt, ts, stt = nc.vector.tensor_tensor, nc.vector.tensor_scalar, nc.vector.scalar_tensor_tensor
            dve.sem_inc(acc_free, 2)

            def lo(g, s, cols):
                dve.wait_ge(hi_ready, 4 * g + (s + 5))
                tt(w_lo[:, s, 0:cols], w_raw[:, s, 0:cols], w_hi[:, s, 0:cols].bitcast(F32), ALU.subtract) \
                    .then_inc(lo_ready, 1)

            def read_result(bank, n):
                dve.wait_ge(S("cross_ready"), n + 1)
                tt(tmp[:], acc[bank][:, 0:T], cross[:, bank], ALU.add).then_inc(acc_free, 1)
                dve.wait_ge(acc_free, n + 3)

            def scaled_result(b, bank, n):
                read_result(bank, n)
                own.link(tt(e_pad[:, b, 2:], tmp[:], rstd[:], ALU.mult))

            def shifted(dst, b, mu, rows=P):
                e, before = e_pad[0:rows, b, 2:], e_pad[0:rows, b, 1:1 + T]
                own.link(tt(tmp[0:rows], before, e, ALU.subtract))
                return stt(out=dst, in0=tmp[0:rows], scalar=mu, in1=e, op0=ALU.mult, op1=ALU.add)

            def split(dst, c, src):
                own.link(nc.vector.tensor_copy(chunk(dst, c), src))
                return tt(chunk(dst, c, T, 2 * T), src, chunk(dst, c).bitcast(F32), ALU.subtract)

            def next_h(which, c, n):
                dve.wait_ge(S("h_hi_ready"), n)
                stt(out=chunk(h, c, T, 2 * T), in0=chunk(x, c), scalar=gain[:, which, bass.ds(c, 1)],
                    in1=chunk(h, c).bitcast(F32), op0=ALU.mult, op1=ALU.subtract).then_inc(S("h_ready"), 1)

            def mean_square(n):
                dve.wait_ge(S("square_sum_ps"), n + 1)
                ts(ms[:], aux[:, 4, 0:T], 1.0 / D, RMS_EPS, ALU.mult, ALU.add).then_inc(S("mean_square_ready"), 1)
                dve.wait_ge(S("rms_ready"), n + 1)
                nc.vector.reciprocal(rstd[:], ms[:]).then_inc(S("rstd_ready"), 1)
                dve.wait_ge(S("rstd_ready"), n + 1)

            dve.wait_ge(params_landed, 16 * N_PARAMS)
            dve.wait_ge(S("consts_ready"), N_CONSTS)
            for s in range(SLOTS):
                lo(-1, s, UA)
            for c in range(2):
                own.link(nc.vector.tensor_copy(mask[:, c].rearrange("p (a b) -> p a b", a=3), mat[:, MASKS:MASKS + 3]))
            ts(mixp[:, :, W0:A0 + 1], mixp[:, :, W0:A0 + 1], 0.5, None, ALU.mult).then_inc(S("halved"), 1)
            with dve.Fori(0, DC) as c:
                next_h(0, c, c + 1)
            mean_square(0)
            for g in range(G_LOW):
                for e in range(2):
                    n = 2 * g + e
                    lo(g, 2 * e, UA)
                    scaled_result(e, n % 2, n)
                    lo(g, 2 * e + 1, UA)
                    if n == 0:
                        rows = slice(LORA, LORA + HEADS)
                        fx, fm = forget[rows, 0], forget[rows, 1]
                        own.link(ts(fx, e_pad[rows, 0, 2:], bf[rows, 0:1], None, ALU.add))
                        stt(out=fm, in0=fx, scalar=-1.0, in1=fx, op0=ALU.mult, op1=ALU.max) \
                            .then_inc(S("forget_abs"), 1)
                    rows = LORA if n < 2 else P
                    ins = shifted(low[0:rows, n], e, mu_low[0:rows, n:n + 1], rows)
                    if n < 3:
                        own.link(ins)
                    else:
                        ins.then_inc(S("low_shifted"), 1)
            dve.wait_ge(S("low_tanh"), 2)
            ts(low[:, 2:4], low[:, 2:4], 0.5, 0.5, ALU.mult, ALU.add).then_inc(S("low_ready"), 1)
            dve.wait_ge(S("forget_ln"), 1)
            rows = slice(LORA, LORA + HEADS)
            own.link(stt(out=forget[rows, 0], in0=forget[rows, 0], scalar=0.0, in1=forget[rows, 1], op0=ALU.min,
                         op1=ALU.subtract))
            own.link(nc.vector.tensor_tensor_scan(forget[rows, 1], ones[rows, 0:1].to_broadcast([HEADS, T]), forget[rows, 0], 0.0, ALU.mult,
                                                  ALU.add))
            ts(forget[rows, 0], forget[rows, 1], -1.0 / ATT_SCALE, None, ALU.mult).then_inc(S("forget_ready"), 1)

            def unit_lo(i, u):
                lo(TILES // 2 * i + (FIRST_IN + u // SLOTS), u % SLOTS, UA)

            def rwkv_result(i, t):
                scaled_result(t % 2, t % 2, TILES * i + (2 * FIRST_IN + t))
                own.link(shifted(rkv[:, t], t % 2, mixp[:, bass.ds(i, 1), MU_R + t]))

            def fox_result(i, t):
                read_result(t % 2, TILES * i + (2 * FIRST_IN + t))
                tt(qkv[:, t - 3], tmp[:], rstd[:], ALU.mult).then_inc(S("qkv_ready"), 1)

            r, k, v = rkv[:, 0], rkv[:, 1], rkv[:, 2]
            halves = lambda t: t.rearrange("p (a b) -> p a b", a=2)

            def key_square(i):
                own.link(ts(kk[:], k, mixp[:, bass.ds(i, 1), K_K], None, ALU.mult))
                tt(kn[:], kk[:], kk[:], ALU.mult).then_inc(S("key_squared"), 1)

            def key_norm(i):
                dve.wait_ge(S("key_norm_ps"), i + 1)
                ts(rs[:], aux[:, 5, 0:T], 1e-24, None, ALU.max).then_inc(S("key_norm_ready"), 1)

            def low_rank(i):
                dve.wait_ge(S("lora_read"), i + 1)
                own.link(ts(log_w[:], log_w[:], -EXP_HALF / 2, -EXP_HALF / 2, ALU.mult, ALU.add))
                a = own.mark(ts(iclr[:], iclr[:], 0.5, 0.5, ALU.mult, ALU.add))
                for c in range(2):
                    scan = own.mark(nc.vector.tensor_tensor_scan(cum[:, c, 1:], ones[:], log_w[:, c * P:c * P + P],
                                                                 0.0, ALU.mult, ALU.add))
                own.done(scan)
                ts(neg_mid[:], cum[:, :, P // 2], -1.0, None, ALU.mult).then_inc(S("cum_ready"), 1)

            def bonus_product(i):
                own.link(ts(y[:], iclr[:], 1.0, mixp[:, bass.ds(i, 1), K_A], ALU.subtract, ALU.mult))
                own.link(stt(out=k, in0=y[:], scalar=1.0, in1=k, op0=ALU.add, op1=ALU.mult))
                stt(out=y_sq[:], in0=r, scalar=mixp[:, bass.ds(i, 1), R_K], in1=k, op0=ALU.mult, op1=ALU.mult) \
                    .then_inc(S("bonus_product"), 1)

            def bonus(i):
                dve.wait_ge(S("bonus_ps"), i + 1)
                tt(chunk(mixed, i), aux[:, 1, 0:T], v, ALU.mult).then_inc(S("bonus_ready"), 1)

            def keys(i):
                dve.wait_ge(S("key_root_ready"), i + 1)
                own.link(nc.vector.reciprocal(rs[:], rs[:]))
                own.link(tt(kk[:], kk[:], rs[:], ALU.mult))
                own.link(stt(out=kn[:], in0=kk[:], scalar=-1.0, in1=iclr[:], op0=ALU.mult, op1=ALU.mult))
                dve.wait_ge(S("decay_ready"), i + 1)
                tt(kinv[:], halves(k), inv_dec[:, :, 1:], ALU.mult)
                tt(binv[:], halves(kn[:]), inv_dec[:, :, 1:], ALU.mult).then_inc(S("keys_ready"), 1)

            def queries(i):
                tt(kr[:, :, 0:P], halves(kk[:]), dec[:, :, 0:P], ALU.mult)
                tt(kr[:, :, P:2 * P], halves(r), dec[:, :, 1:], ALU.mult).then_inc(S("queries_ready"), 1)

            def masked_grams(j):
                dve.wait_ge(S("grams_ps"), 2 * j + 2)
                tt(state_scale[:], dec[:, 0, P:P + 1], inv_dec[:, 1, 0:1], ALU.mult)
                for hd in range(2):
                    nc.vector.copy_predicated(al[:, 2 * hd:2 * hd + 2], mask[:, :, 2 * P:],
                                              aux[:, 4 + hd, 0:2 * P].rearrange("p (a b) -> p a b", a=2)) \
                        .then_inc(S("al_masked"), 1)
                for hd in range(2):
                    nc.vector.copy_predicated(abr[:, 2 * hd:2 * hd + 2], mask[:, :, 0:2 * P],
                                              aux[:, 2 + hd].rearrange("p (a b) -> p a b", a=2)) \
                        .then_inc(S("abr_masked"), 1)
                dve.wait_ge(S("al_masked"), 2 * j + 2)
                low_blocks = own.mark(tt(inv[:, 1], al[:], mat_b(ONE_LOW, 4), ALU.mult))
                dve.wait_ge(S("abr_masked"), 2 * j + 2)
                up_blocks = own.mark(tt(inv[:, 0], abr[:, :, 0:P], mat_b(ONE_UP, 4), ALU.mult))
                own.done(low_blocks)
                tt(inv[:, 1], inv[:, 1], mat_b(IDENT, 4), ALU.add)
                own.done(up_blocks)
                tt(inv[:, 0], inv[:, 0], mat_b(IDENT, 4), ALU.add).then_inc(S("inv_ready"), 1)
                for hd in range(2):
                    nc.vector.copy_predicated(akr[:, 2 * hd:2 * hd + 2], mask[:, :, 0:2 * P],
                                              aux[:, hd].rearrange("p (a b) -> p a b", a=2)) \
                        .then_inc(S("akr_masked"), 1)

            def doubled(j, lv):
                dve.wait_ge(S("inv_ps"), LEVELS * j + (lv + 1))
                dve.wait_ge(S("inv_ready"), (LEVELS + 1) * j + (lv + 1))
                n = 2 if lv < LEVELS - 1 else 1
                tt(inv[:, 0:n], inv[:, 0:n], aux[:, 2:2 + n].rearrange("p m (a b) -> p m a b", a=4), ALU.add) \
                    .then_inc(S("inv_ready"), 1)

            def next_state(j):
                dve.wait_ge(S("state_ps"), j + 1)
                stt(out=state[:], in0=aux[:, 2, 0:P], scalar=state_scale[:], in1=mat[:, HEAD_BLOCKS], op0=ALU.mult,
                    op1=ALU.mult).then_inc(S("state_ready"), 1)

            def centred(j):
                dve.wait_ge(S("mean_ps"), j + 1)
                stt(out=y[:], in0=aux[:, 2, 0:T], scalar=-1.0 / 64, in1=y[:], op0=ALU.mult, op1=ALU.add) \
                    .then_inc(S("y_centred"), 1)

            def variance(j):
                dve.wait_ge(S("var_ps"), j + 1)
                ts(var[:], aux[:, 0, 0:T], 1.0 / 64, GN_EPS, ALU.mult, ALU.add).then_inc(S("var_ready"), 1)

            def normed(j):
                dve.wait_ge(S("group_root_ready"), j + 1)
                own.link(nc.vector.reciprocal(var[:], var[:]))
                tt(y[:], y[:], var[:], ALU.mult).then_inc(S("y_scaled"), 1)

            def gated(j):
                dve.wait_ge(S("group_norm_ready"), j + 1)
                own.link(tt(y[:], y[:], chunk(mixed, j), ALU.add))
                dve.wait_ge(S("gate_read"), j + 1)
                tt(chunk(mixed, j), y[:], gate[:], ALU.mult).then_inc(S("rwkv_done"), 1)

            def scores(n):
                dve.wait_ge(S("scores_ps"), n + 1)
                first = own.mark(tt(prob[:, 0:P], aux[:, 1, 0:P], mat[:, CAUSAL], ALU.add))
                own.mark(nc.vector.tensor_copy(prob[:, P:2 * P], aux[:, 1, P:2 * P]))
                second = own.mark(tt(prob[:, 2 * P:], aux[:, 1, 2 * P:3 * P], mat[:, CAUSAL], ALU.add))
                own.done(first)
                own.mark(nc.vector.tensor_reduce(row_max[:, 0:1], prob[:, 0:P], AX.X, ALU.max))
                own.done(second)
                own.link(nc.vector.tensor_reduce(row_max[:, 1:2], prob[:, P:], AX.X, ALU.max))
                ts(row_max, row_max, -ATT_SCALE, None, ALU.mult).then_inc(S("scores_ready"), 1)

            def probabilities(n):
                dve.wait_ge(S("exp_ready"), n + 1)
                own.link(nc.vector.reciprocal(row_sum, row_sum))
                ts(prob[:, 0:P], prob[:, 0:P], row_sum[:, 0:1], None, ALU.mult)
                ts(prob[:, P:], prob[:, P:], row_sum[:, 1:2], None, ALU.mult).then_inc(S("probs_ready"), 1)

            def attended(n):
                dve.wait_ge(S("attn_ps"), n + 1)
                nc.vector.tensor_copy(chunk(mixed, n + PAIRS), aux[:, 1, 0:T]).then_inc(S("attn_done"), 1)

            def body(i, mix, load):
                j = i - 1
                if mix:
                    masked_grams(j)
                if load:
                    unit_lo(i, 0)
                    rwkv_result(i, 0)
                    unit_lo(i, 1)
                if mix:
                    doubled(j, 0)
                if load:
                    unit_lo(i, 2)
                if mix:
                    scores(j)
                    doubled(j, 1)
                if load:
                    rwkv_result(i, 1)
                    unit_lo(i, 3)
                if mix:
                    probabilities(j)
                    doubled(j, 2)
                if load:
                    unit_lo(i, 4)
                if mix:
                    doubled(j, 3)
                    attended(j)
                if load:
                    rwkv_result(i, 2)
                    key_square(i)
                    unit_lo(i, 5)
                if mix:
                    doubled(j, 4)
                if load:
                    low_rank(i)
                    unit_lo(i, 6)
                if mix:
                    doubled(j, 5)
                if load:
                    key_norm(i)
                    fox_result(i, 3)
                    bonus_product(i)
                    unit_lo(i, 7)
                if mix:
                    next_state(j)
                if load:
                    unit_lo(i, 8)
                    bonus(i)
                    fox_result(i, 4)
                    keys(i)
                    unit_lo(i, 9)
                if mix:
                    centred(j)
                if load:
                    queries(i)
                    unit_lo(i, 10)
                if mix:
                    variance(j)
                if load:
                    fox_result(i, 5)
                    rows = slice(LORA, LORA + HEADS)
                    ts(forget_sel[rows], forget[rows, 0], mat[rows, IDENT, bass.ds(i + LORA, 1)], None, ALU.mult) \
                        .then_inc(S("qkv_ready"), 1)
                if mix:
                    normed(j)
                if load:
                    unit_lo(i, 11)
                if mix:
                    gated(j)

            body(0, False, True)
            with own.loop(PAIRS, 29, start=1) as i:
                body(i, True, True)
            body(PAIRS, True, False)

            with dve.Fori(0, PAIRS + HEADS) as c:
                dve.wait_ge(S("mixed_hi_ready"), c + 1)
                tt(chunk(act_in, c, T, 2 * T), chunk(mixed, c), chunk(act_in, c).bitcast(F32), ALU.subtract) \
                    .then_inc(S("mixed_ready"), 1)

            def add_to_x(c, bank, n, final):
                read_result(bank, n)
                ins = tt(chunk(x, c), chunk(x, c), tmp[:], ALU.add)
                if final is not None:
                    ins.then_inc(x_done, 1)
                    dve.wait_ge(x_done, final)
                else:
                    own.link(ins)

            with own.loop(G_OUT, 0) as i:
                for e in range(2):
                    lo(i + FIRST_OUT, 2 * e, UA)
                    add_to_x(2 * i + e, e, 2 * i + (2 * FIRST_OUT + e), 2 * i + (e + 1))
                    lo(i + FIRST_OUT, 2 * e + 1, UA)
                    next_h(2, 2 * i + e, 2 * i + (DC + e + 1))
            mean_square(1)

            def taps(conv, e, k):
                return stt(out=u_t[:, e], in0=e_pad[:, e, k:k + T], scalar=convp[:, bass.ds(conv + e, 1), k],
                           in1=u_t[:, e], op0=ALU.mult, op1=ALU.add)

            def scaled(pair, e, n):
                read_result(e, n)
                tt(e_pad[:, e, 2:], tmp[:], rstd[:], ALU.mult).then_inc(S("scaled_ready"), 1)

            def up_pair(g, n, pair, c, conv, cols, first=False):
                if not first:
                    rest_taps(pair - 1, conv - 2)
                lo(g, 0, cols)
                if not first:
                    rest_product(pair - 1)
                scaled(pair, 0, n)
                if not first:
                    rest_lo(pair - 1, c - 1)
                lo(g, 1, cols)
                dve.wait_ge(S("tap_ready"), 2 * pair + 1)
                own.link(taps(conv, 0, 1))
                taps(conv, 0, 0).then_inc(S("gate_ready"), 1)
                lo(g, 2, cols)
                scaled(pair, 1, n + 1)
                lo(g, 3, cols)

            def rest_taps(pair, conv):
                dve.wait_ge(S("tap_ready"), 2 * pair + 2)
                t = own.mark(taps(conv, 1, 1))
                dve.wait_ge(S("tanh_ready"), pair + 1)
                own.mark(stt(out=u_t[:, 2], in0=u_t[:, 2], scalar=1.0, in1=u_t[:, 0], op0=ALU.add, op1=ALU.mult))
                own.done(t)
                own.value = own.mark(taps(conv, 1, 0))

            def rest_product(pair):
                own.done(own.value)
                stt(out=u_t[:, 3], in0=u_t[:, 2], scalar=0.5, in1=u_t[:, 1], op0=ALU.mult, op1=ALU.mult) \
                    .then_inc(S("product_ready"), 1)

            def rest_lo(pair, c):
                dve.wait_ge(S("feature_hi_ready"), pair + 1)
                tt(chunk(act_in, c, T, 2 * T), u_t[:, 3], chunk(act_in, c).bitcast(F32), ALU.subtract) \
                    .then_inc(S("features_ready"), 1)

            for layer in range(2):
                dve.wait_ge(S("rstd_ready"), 2 + 2 * layer)
                g0, n0, p0 = FIRST_FFN[layer], R_FFN[layer], layer * QUARTERS * G_UP
                for q in range(QUARTERS):
                    final = q == QUARTERS - 1
                    last = G_UP - 1
                    up_pair(g0, n0, p0, 0, 2 * p0, UA, first=True)
                    with own.loop(last, 4, start=1) as i:
                        up_pair(i + g0, 2 * i + n0, i + p0, i, 2 * i + 2 * p0, UA)
                    up_pair(g0 + last, n0 + 2 * last, p0 + last, last, 2 * (p0 + last), UB)
                    rest_taps(p0 + last, 2 * (p0 + last))
                    rest_product(p0 + last)
                    rest_lo(p0 + last, last)
                    g1, n1 = g0 + G_UP, n0 + 2 * G_UP

                    def down_group(i, cols):
                        for s in range(SLOTS):
                            if cols:
                                lo(i + g1, s, cols)
                            add_to_x(4 * i + s, s % 2, 4 * i + (n1 + s),
                                     4 * i + (DC * (1 + 2 * layer) + s + 1) if final else None)

                    with own.loop(G_DOWN - 1, 0 if final else 4) as i:
                        down_group(i, UB)
                    down_group(G_DOWN - 1, None if final and layer == 1 else UA)
                    g0, n0, p0 = g0 + G_QUARTER, n0 + R_QUARTER, p0 + G_UP
                mean_square(2 + 2 * layer)
                if layer == 0:
                    pooling(nc, dve, own, S, x, gain, rstd, win, invc, act_in, split)
                    for i in range(G_POOL):
                        for s in range(SLOTS):
                            lo(FIRST_POOL + i, s, UA)
                            for r in range(2):
                                c = 8 * i + 2 * s + r
                                read_result(r, R_POOL + c)
                                stt(out=x[:, c], in0=tmp[:], scalar=poolp[:, c:c + 1], in1=x[:, c], op0=ALU.mult,
                                    op1=ALU.add).then_inc(x_done, 1)
                                dve.wait_ge(x_done, 2 * DC + c + 1)
                                next_h(3, c, 2 * DC + c + 1)
                    mean_square(3)
            dve.wait_ge(S("rstd_ready"), 5)
            with dve.Fori(0, DC) as c:
                stt(out=chunk(x, c), in0=chunk(x, c), scalar=gain[:, 4, bass.ds(c, 1)], in1=rstd[:], op0=ALU.mult,
                    op1=ALU.mult).then_inc(S("out_ready"), 1)

        @block.tensor
        def _(pe):
            mm = nc.tensor.matmul

            def block_product(bank, s, b, rhs, start, stop):
                cols = slice(b * P, b * P + P)
                mm(acc[bank][:], w_hi[:, s, cols], rhs, start=start, stop=False, skip_group_check=True)
                return mm(acc[bank][:, 0:T], w_lo[:, s, cols], rhs[:, 0:T], start=False, stop=stop,
                          skip_group_check=True)

            def tile(g, e, bank, n, src, ready, count, between=None):
                pe.wait_ge(acc_free, n + 1)
                for half in range(2):
                    s = 2 * e + half
                    pe.wait_ge(lo_ready, 4 * g + (s + 1))
                    pe.wait_ge(ready, count - (8 if half == 0 else 1))
                    for b in range(8):
                        c = 8 * half + b
                        if c == DC - 1:
                            pe.wait_ge(ready, count)
                        ins = block_product(bank, s, b, src[:, c], c == 0, c == DC - 1)
                    ins.then_inc(units_done, 1)
                    if half == 0 and between is not None:
                        square_sum(between)

            def square_sum(n):
                pe.wait_ge(S("summed"), DC * (n + 1))
                mm(aux[:, 4, 0:T], ones[:], ssum[:], start=True, stop=True).then_inc(S("square_sum_ps"), 1)

            pe.wait_ge(params_landed, 16 * N_PARAMS)
            for g in range(G_LOW):
                for e in range(2):
                    tile(g, e, e, 2 * g + e, h, S("h_ready"), DC, 0 if g == e == 0 else None)

            heads = [slice(64 * hd, 64 * hd + 64) for hd in range(2)]

            def part(i, t, first, last, load=True):
                if not load:
                    return
                g, e = TILES // 2 * i + (FIRST_IN + t // 2), t % 2
                if first == 0:
                    pe.wait_ge(acc_free, TILES * i + (2 * FIRST_IN + t + 1))
                for c in range(first, last):
                    if c % 8 == 0:
                        pe.wait_ge(lo_ready, 4 * g + (2 * e + c // 8 + 1))
                    ins = block_product(e, 2 * e + c // 8, c % 8, h[:, c], c == 0, c == DC - 1)
                    if c % 8 == 7:
                        ins.then_inc(units_done, 1)

            def low_rank(i):
                pe.wait_ge(S("lora_landed"), 16 * i + 16)
                mm(aux[:, 4, 0:T], lora_w[0:LORA, 0], low[0:LORA, 0], start=True, stop=True)
                mm(aux[:, 4, T:2 * T], lora_w[0:LORA, 1], low[0:LORA, 1], start=True, stop=True) \
                    .then_inc(S("lora_ps"), 1)

            def key_norm(i):
                pe.wait_ge(S("key_squared"), i + 1)
                mm(aux[:, 5, 0:T], mat[:, HEAD_BLOCKS], kn[:], start=True, stop=True).then_inc(S("key_norm_ps"), 1)

            def bonus(i):
                pe.wait_ge(S("bonus_product"), i + 1)
                mm(aux[:, 1, 0:T], mat[:, HEAD_BLOCKS], y_sq[:], start=True, stop=True).then_inc(S("bonus_ps"), 1)

            def turned(i):
                pe.wait_ge(S("keys_ready"), i + 1)
                for k, src in enumerate((rkv[:, 2, 0:P], rkv[:, 2, P:T], kinv[:, 0], binv[:, 0])):
                    ins = nc.tensor.transpose(aux[:, 4, k * P:k * P + P], src, mat[:, IDENT])
                ins.then_inc(S("turned_ps"), 1)

            def grams(j):
                pe.wait_ge(S("queries_ready"), j + 1)
                pe.wait_ge(S("tok_ready"), j + 1)
                pe.wait_ge(S("bonus_ready"), j + 1)
                for c in range(2):
                    for hd, ch in enumerate(heads):
                        ins = mm(aux[:, 4 + hd, c * P:c * P + P], kr[ch, c, 0:P], binv[ch, c], start=True, stop=True)
                ins.then_inc(S("grams_ps"), 1)
                for k, bank in ((binv, 2), (kinv, 0)):
                    if bank == 0:
                        pe.wait_ge(S("qkv_ready"), 4 * j + 4)
                    for c in range(2):
                        for hd, ch in enumerate(heads):
                            ins = mm(aux[:, bank + hd, c * 2 * P:(c + 1) * 2 * P], k[ch, c], kr[ch, c], start=True,
                                     stop=True)
                ins.then_inc(S("grams_ps"), 1)

            def w1_level(j, lv):
                pe.wait_ge(S("off_ready"), LEVELS * j + (lv + 1))
                pe.wait_ge(S("inv_ready"), (LEVELS + 1) * j + (lv + 1))
                if lv == 0:
                    pe.wait_ge(S("akr_masked"), 2 * j + 2)
                for p in range(4):
                    ins = mm(aux[:, 0, p * P:p * P + P], off[:, p], inv[:, 0, p], start=True, stop=True)
                ins.then_inc(S("w1_ps"), 1)

            def inv_level(j, lv):
                pe.wait_ge(S("w1_ready"), LEVELS * j + (lv + 1))
                for p in range(4):
                    ins = mm(aux[:, 2, p * P:p * P + P], inv[:, 1, p], w1[:, p], start=True, stop=True)
                if lv < LEVELS - 1:
                    for p in range(4):
                        ins = mm(aux[:, 3, p * P:p * P + P], w1[:, p], inv[:, 1, p], start=True, stop=True)
                ins.then_inc(S("inv_ps"), 1)

            def right_side(j, c):
                if c:
                    pe.wait_ge(S("state_ready"), j + 1)
                    mm(aux[:, 0, 0:P], kr[:, 1, 0:P], state[:], start=True, stop=False, skip_group_check=True)
                for hd, v in enumerate(heads):
                    ins = mm(aux[:, 0, v], akr[:, 2 * hd + c, 0:P], tok[:, c, v], start=c == 0, stop=True,
                             skip_group_check=True)
                ins.then_inc(S("ru_ps"), 1)

            def solution(j, c):
                if c == 0:
                    pe.wait_ge(S("inv_ready"), (LEVELS + 1) * j + (LEVELS + 1))
                pe.wait_ge(S("ru_ready"), 4 * j + (2 * c + 1))
                for hd, v in enumerate(heads):
                    ins = mm(aux[:, 0, v], inv[:, 0, 2 * hd + c], ru[:, 0, v], start=True, stop=True)
                ins.then_inc(S("ru_ps"), 1)

            def outputs(j, c):
                pe.wait_ge(S("ru_ready"), 4 * j + (2 * c + 2))
                if c == 0:
                    mm(aux[:, 2, 0:P], tok[:, 2], tok[:, 0], start=True, stop=False)
                    mm(aux[:, 2, 0:P], tok[:, 3], ru[:, 1], start=False, stop=True).then_inc(S("state_ps"), 1)
                else:
                    mm(aux[:, 3, P:T], state[:], kr[:, 1, P:2 * P], start=True, stop=False, skip_group_check=True)
                for hd, v in enumerate(heads):
                    dst = aux[v, 3, c * P:c * P + P]
                    mm(dst, tok[:, c, v], akr[:, 2 * hd + c, P:2 * P], start=c == 0, stop=False, skip_group_check=True)
                    ins = mm(dst, ru[:, 1, v], abr[:, 2 * hd + c, P:2 * P], start=False, stop=True,
                             skip_group_check=True)
                if c:
                    ins.then_inc(S("y_ps"), 1)

            def mean_and_gate(j):
                pe.wait_ge(S("y_ready"), j + 1)
                mm(aux[:, 2, 0:T], mat[:, HEAD_BLOCKS], y[:], start=True, stop=True).then_inc(S("mean_ps"), 1)
                pe.wait_ge(S("gate_landed"), 16 * j + 16)
                mm(aux[:, 3, 0:T], gate_w[:, 0], low[:, 2], start=True, stop=False)
                mm(aux[:, 3, 0:T], gate_w[:, 1], low[:, 3], start=False, stop=True).then_inc(S("gate_ps"), 1)

            def square_mean(j):
                pe.wait_ge(S("y_squared"), j + 1)
                mm(aux[:, 0, 0:T], mat[:, HEAD_BLOCKS], y_sq[:], start=True, stop=True).then_inc(S("var_ps"), 1)

            def scores(n):
                pe.wait_ge(S("qkv_ready"), 4 * n + 4)
                q, k = qkv[:, 0], qkv[:, 1]
                mm(aux[:, 1, 0:P], q[:, 0:P], k[:, 0:P], start=True, stop=False)
                mm(aux[:, 1, 0:P], ones[:], forget_sel[:, 0:P], start=False, stop=True)
                mm(aux[:, 1, P:3 * P], q[:, P:T], k, start=True, stop=False)
                mm(aux[:, 1, P:3 * P], ones[:], forget_sel[:], start=False, stop=True).then_inc(S("scores_ps"), 1)

            def fox_turned(n):
                pe.wait_ge(S("probs_ready"), n + 1)
                for b in range(3):
                    nc.tensor.transpose(aux[:, 4, b * P:b * P + P], prob[:, b * P:b * P + P], mat[:, IDENT])
                for b in range(2):
                    ins = nc.tensor.transpose(aux[:, 5, b * P:b * P + P], qkv[:, 2, b * P:b * P + P], mat[:, IDENT])
                ins.then_inc(S("fox_turned_ps"), 1)

            def attended(n):
                pe.wait_ge(S("fox_turned"), n + 1)
                mm(aux[:, 1, 0:P], v_tok[:, 0:P], prob_t[:, 0:P], start=True, stop=True)
                mm(aux[:, 1, P:T], v_tok[:, 0:P], prob_t[:, P:2 * P], start=True, stop=False)
                mm(aux[:, 1, P:T], v_tok[:, P:2 * P], prob_t[:, 2 * P:3 * P], start=False, stop=True) \
                    .then_inc(S("attn_ps"), 1)

            def body(i, mix, load):
                j = i - 1
                if mix:
                    grams(j)
                part(i, 0, 0, 16, load)
                part(i, 1, 0, 4, load)
                steps = (
                    (((1, 4, 8),), scores, ((1, 8, 11),)),
                    (((1, 11, 15),), None, ((1, 15, 16), (2, 0, 4))),
                    (((2, 4, 8),), fox_turned, ((2, 8, 11),)),
                    (((2, 11, 15),), attended, ((2, 15, 16), (3, 0, 3))),
                    (((3, 3, 7),), None, ((3, 7, 10),)),
                    (((3, 10, 14),), None, ()))
                for lv, (blocks, attention, more) in enumerate(steps):
                    if mix:
                        w1_level(j, lv)
                    for b in blocks:
                        part(i, *b, load)
                    if mix:
                        inv_level(j, lv)
                        if attention is not None:
                            attention(j)
                    if load and lv == 4:
                        low_rank(i)
                    for b in more:
                        part(i, *b, load)
                if mix:
                    right_side(j, 0)
                if load:
                    key_norm(i)
                part(i, 3, 14, 16, load)
                part(i, 4, 0, 3, load)
                if mix:
                    solution(j, 0)
                part(i, 4, 3, 7, load)
                if load:
                    bonus(i)
                if mix:
                    outputs(j, 0)
                part(i, 4, 7, 13, load)
                if mix:
                    right_side(j, 1)
                part(i, 4, 13, 16, load)
                if mix:
                    solution(j, 1)
                part(i, 5, 0, 4, load)
                if mix:
                    outputs(j, 1)
                part(i, 5, 4, 8, load)
                if mix:
                    mean_and_gate(j)
                part(i, 5, 8, 11, load)
                if mix:
                    square_mean(j)
                if load:
                    turned(i)
                part(i, 5, 11, 16, load)

            pe.wait_ge(S("low_ready"), 1)
            body(0, False, True)
            with pe.Fori(1, PAIRS) as i:
                body(i, True, True)
            body(PAIRS, True, False)

            with pe.Fori(0, G_OUT) as i:
                for e in range(2):
                    tile(i + FIRST_OUT, e, e, 2 * i + (2 * FIRST_OUT + e), act_in, S("mixed_ready"), DC)

            for layer in range(2):
                g0, n0, f0 = FIRST_FFN[layer], R_FFN[layer], layer * QUARTERS * G_UP
                for q in range(QUARTERS):
                    def up(i, between=None):
                        for e in range(2):
                            tile(i + g0, e, e, 2 * i + (n0 + e), h, S("h_ready"), DC * (layer + 2),
                                 between if e == 0 else None)
                    if q == 0:
                        up(0, 1 + 2 * layer)
                        with pe.Fori(1, G_UP) as i:
                            up(i)
                    else:
                        with pe.Fori(0, G_UP) as i:
                            up(i)
                    with pe.Fori(0, G_DOWN) as i:
                        for s in range(SLOTS):
                            pe.wait_ge(acc_free, 4 * i + (n0 + 2 * G_UP + s + 1))
                            pe.wait_ge(lo_ready, 4 * i + (4 * (g0 + G_UP) + s + 1))
                            pe.wait_ge(S("features_ready"), f0 + G_UP - 1)
                            for b in range(FC):
                                if b == FC - 1:
                                    pe.wait_ge(S("features_ready"), f0 + G_UP)
                                ins = block_product(s % 2, s, b, act_in[:, b], b == 0, b == FC - 1)
                            ins.then_inc(units_done, 1)
                    g0, n0, f0 = g0 + G_QUARTER, n0 + R_QUARTER, f0 + G_UP
                square_sum(2 + 2 * layer)
                if layer == 0:
                    for i in range(G_POOL):
                        for s in range(SLOTS):
                            u = 4 * i + s
                            pe.wait_ge(lo_ready, 4 * (FIRST_POOL + i) + s + 1)
                            pe.wait_ge(S("pooled_ready"), 4 * (u // 2) + 4)
                            for r in range(2):
                                pe.wait_ge(acc_free, R_POOL + 2 * u + r + 1)
                                for b in range(4):
                                    ins = block_product(r, s, 4 * r + b, act_in[:, 4 * (u // 2) + b], b == 0, b == 3)
                            ins.then_inc(units_done, 1)


N_CONSTS, N_PARAMS = 7, 7


def pooling(nc, dve, own, S, x, gain, rstd, win, invc, act_in, split):
    tt, stt = nc.vector.tensor_tensor, nc.vector.scalar_tensor_tensor
    nc.vector.memset(win[:, :, 0:16], 0.0).then_inc(S("win_cleared"), 1)
    dve.wait_ge(S("win_cleared"), 1)
    dve.wait_ge(S("counts_landed"), 16)
    dve.wait_ge(S("rstd_ready"), 3)
    for g in range(len((2, 4, 8, 16))):
        with own.loop(4, 5 + g) as i:
            c = i + 4 * g
            own.link(stt(out=win[:, 0, 16:], in0=chunk(x, c), scalar=gain[:, 1, bass.ds(c, 1)], in1=rstd[:],
                         op0=ALU.mult, op1=ALU.mult))
            src = 0
            for k in range(g + 1):
                dst = 1 + k % 2
                own.link(tt(win[:, dst, 16:], win[:, src, 16:], win[:, src, 16 - 2 ** k:16 - 2 ** k + T], ALU.add))
                src = dst
            own.link(tt(win[:, src, 16:], win[:, src, 16:], invc[:, g], ALU.mult))
            own.link(tt(win[:, src, 16:], win[:, src, 16:], win[:, 0, 16:], ALU.subtract))
            split(act_in, c, win[:, src, 16:]).then_inc(S("pooled_ready"), 1)


def _tables():
    import numpy as np
    row, col = np.arange(P)[:, None], np.arange(P)[None, :]
    low = lambda b: (row // (2 * b) == col // (2 * b)) & (row // b % 2 == 1) & (col // b % 2 == 0)
    mats = [low(2 ** (lv + 1)) for lv in range(LEVELS)] + [low(1), low(1).T, row == col, row // 64 == col // 64]
    mats += [np.where(row >= col, 0, -1e30), row < col, row <= col, row > col]
    mats = np.stack([m.astype(np.float32) for m in mats], 1)
    t = np.arange(T)
    count = np.stack([(1 / np.minimum(t + 1, w)).astype(np.float32) for w in (2, 4, 8, 16)])
    return mats, np.broadcast_to(count, (P, 4, T)).copy()


def _layouts(a):
    import numpy as np
    f = {k: np.asarray(v) for k, v in a.items()}
    cols = lambda v: np.ascontiguousarray(v.reshape(-1, P).T)

    def halves(w):
        m = w.shape[1] // P
        return w.reshape(2, 8, P, m, P).transpose(3, 0, 2, 1, 4).reshape(2 * m, P, UA)

    def pad(v, n=P):
        return np.concatenate([v, np.zeros(v.shape[:-1] + (n - v.shape[-1],), v.dtype)], -1)

    W = HEADS * P
    fox, rw = 3 * W + HEADS, 3 * W
    w_in, mu = f["w_in"][0], f["shift_mu"][0]
    wd, ad, gd = fox + rw, fox + rw + LORA, fox + rw + 2 * LORA
    order = [pad(np.concatenate([w_in[:, ad:ad + LORA], w_in[:, 3 * W:fox]], 1)), pad(w_in[:, wd:wd + LORA]),
             w_in[:, gd:]]
    for j in range(PAIRS):
        order += [w_in[:, first + k * W + j * P:first + k * W + j * P + P] for first in (fox, 0) for k in range(3)]
    w_out = np.concatenate([f["w_out"][0][W:], f["w_out"][0][:W]], 0)
    pool = f["w_pool"][0].reshape(4, 4, P, 2, 2, P).transpose(0, 3, 2, 4, 1, 5).reshape(8, P, UA)
    ups = [halves(w.reshape(D, 2, D_FF // P, P).transpose(0, 2, 1, 3).reshape(D, 2 * D_FF)) for w in f["w_ffn_up"]]
    wa = np.concatenate([halves(np.concatenate(order, 1)), halves(w_out), ups[0], pool, ups[1]], 0)
    wb = np.concatenate([w.reshape(QUARTERS, FC, P, DC, P).transpose(0, 3, 2, 1, 4).reshape(QUARTERS * DC, P, UB)
                         for w in f["w_ffn_down"]], 0)
    mix = np.stack([cols(v) for v in (mu[0:W], mu[W:2 * W], mu[2 * W:3 * W], f["w0"][0], f["a0"][0], f["k_k"][0],
                                      f["k_a"][0], f["r_k"][0].reshape(-1), f["gn_w"][0], f["gn_b"][0])], 2)
    wd, ad, gd = rw, rw + LORA, rw + 2 * LORA
    mu0 = np.stack([pad(mu[ad:ad + LORA]), pad(mu[wd:wd + LORA]), mu[gd:gd + P], mu[gd + P:gd + 2 * P]], 1)
    b_f = np.zeros((P, 1), np.float32)
    b_f[LORA:LORA + HEADS, 0] = f["b_f"][0]
    rows = lambda w: pad(w.T).T.reshape(P, PAIRS, P).transpose(1, 0, 2)
    gate = f["w_gate_up"][0].reshape(2, P, PAIRS, P).transpose(2, 1, 0, 3)
    lora = np.concatenate([rows(f["w_iclr_up"][0])[:, :, None], rows(f["w_decay_up"][0])[:, :, None], gate], 2)
    lora = np.concatenate([lora, np.zeros((1,) + lora.shape[1:], lora.dtype)], 0)
    conv = np.concatenate([f["conv_w"], f["conv_b"][:, None]], 1)
    conv = conv.reshape(2, 4, 2, D_FF // P, P).transpose(4, 0, 3, 2, 1).reshape(P, -1, 4)
    gains = np.stack([cols(v) for v in (f["mix_norm"][0], f["pool_norm"][0], f["ffn_norm"][0], f["ffn_norm"][1],
                                        f["final_norm"])], 1)
    x = f["x"][0].T.reshape(DC, P, T).transpose(1, 0, 2)
    mats, count = _tables()
    named = dict(x_in=x, gains=gains, wa=wa, wb=wb, mix_p=mix, mu0=mu0, b_f=b_f, lora=lora, conv_p=conv,
                 pool_p=cols(f["pool_scale"][0]), mats=mats, inv_count=count)
    return {k: np.ascontiguousarray(v) for k, v in named.items()}


def kernel(**inputs):
    import concourse.bacc as _bacc
    from concourse.bass_utils import run_bass_kernel_spmd as _run

    nc = _bacc.Bacc("TRN2", target_bir_lowering=False, num_devices=1)
    arrays = _layouts(inputs)
    args = {k: nc.dram_tensor(f"{k}_dram", v.shape, mybir.dt.from_np(v.dtype), kind="ExternalInput").ap()
            for k, v in arrays.items()}
    out = nc.dram_tensor("out_dram", (P, DC, T), F32, kind="ExternalOutput").ap()
    trunk(nc, out=out, **args)
    r = _run(nc, [{f"{k}_dram": v for k, v in arrays.items()}], core_ids=[0])
    return r.results[0]["out_dram"].transpose(2, 1, 0).reshape(1, T, D)
```

```python
from contextlib import ExitStack, contextmanager

import concourse.bass as bass
from concourse import mybir

F32 = mybir.dt.float32
F32R = mybir.dt.float32r
U8 = mybir.dt.uint8
ALU = mybir.AluOpType
ACT = mybir.ActivationFunctionType
AX = mybir.AxisListType

P = 128
T = 256
D = 2048
DC = D // P
HEADS = 8
PAIRS = 8
LORA = 96
D_FF = 5632
QUARTERS = 4
FC = D_FF // P // QUARTERS
RMS_EPS = 1e-6
GN_EPS = 64e-5
EXP_HALF = 0.6065306597126334
ATT_SCALE = P ** -0.5
SLOTS = 4
UA = 8 * P
UB = FC * P
LEVELS = 6

MU_R, MU_K, MU_V, W0, A0, K_K, K_A, R_K, GN_W, GN_B = range(10)
ONE_LOW, ONE_UP, IDENT, HEAD_BLOCKS, CAUSAL, MASKS = 6, 7, 8, 9, 10, 11
TILES = 6
G_LOW, G_IN, G_OUT = 2, PAIRS * TILES // 2, DC // 2
MIX_ORDER = (*range(PAIRS - 1), *range(PAIRS, PAIRS + HEADS), PAIRS - 1)
G_UP, G_DOWN, G_POOL = FC, DC // SLOTS, 2
G_QUARTER = G_UP + G_DOWN
FIRST_IN = G_LOW
FIRST_OUT = FIRST_IN + G_IN
FIRST_FFN0 = FIRST_OUT + G_OUT
FIRST_POOL = FIRST_FFN0 + QUARTERS * G_QUARTER
FIRST_FFN1 = FIRST_POOL + G_POOL
FIRST_FFN = (FIRST_FFN0, FIRST_FFN1)
R_QUARTER = 2 * G_UP + 4 * G_DOWN
R_OUT = 2 * FIRST_OUT
R_FFN0 = R_OUT + 2 * DC
R_POOL = R_FFN0 + QUARTERS * R_QUARTER
R_FFN = (R_FFN0, R_POOL + DC)
SECOND_OUT = FIRST_OUT + G_OUT // 2


class Chain:

    def __init__(self, eng, sem):
        self.eng, self.sem, self.base, self.k = eng, sem, 0, 0

    def link(self, ins):
        self.k += 1
        ins.then_inc(self.sem, 1)
        self.eng.wait_ge(self.sem, self.base + self.k)

    def mark(self, ins):
        self.k += 1
        ins.then_inc(self.sem, 1)
        return self.base + self.k

    def done(self, count):
        self.eng.wait_ge(self.sem, count)

    @contextmanager
    def loop(self, count, per, start=0):
        base = self.base + self.k
        with self.eng.Fori(start, count) as i:
            self.base, self.k = per * i + (base - per * start), 0
            yield i
            assert self.k == per, (self.k, per)
        self.base, self.k = base + per * (count - start), 0


def chunk(t, c, lo=0, hi=T):
    return t[:, bass.ds(c, 1), lo:hi].rearrange("p o t -> p (o t)")


def half_blocks(t, lv, odd):
    return t.rearrange("p (n two b) -> p n two b", two=2, b=2 ** (lv + 1))[:, :, odd]


def trunk(nc, x_in, gains, wa, wb, mix_p, mu0, b_f, lora, conv_p, pool_p, mats, inv_count, out):
    with ExitStack() as ctx:
        def sb(name, shape, dt=F32):
            return ctx.enter_context(nc.sbuf_tensor(name, shape, dt))

        def sem(name):
            return ctx.enter_context(nc.semaphore(name))

        x = sb("x", [P, DC, T])
        scope = ExitStack()

        def shared(name, shape, dt=F32):
            return scope.enter_context(nc.sbuf_tensor(name, shape, dt))

        pooled = shared("pooled", [P, DC, 16 + T])
        scope.close()
        h = sb("h", [P, DC, 2 * T], F32R)
        w_raw = sb("w_raw", [P, SLOTS, UB])
        w_hi = sb("w_hi", [P, SLOTS, UB], F32R)
        w_lo = sb("w_lo", [P, SLOTS, UB], F32R)
        gain = sb("gain", [P, 5, DC])
        mixp = sb("mixp", [P, PAIRS, 10])
        mu_low = sb("mu_low", [P, 4])
        bf = sb("bf", [P, 1])
        convp = sb("convp", [P, 2 * 2 * FC * QUARTERS, 4])
        poolp = sb("poolp", [P, DC])
        mask = sb("mask", [P, 2, 3 * P], U8)
        mat = sb("mat", [P, 14, P])
        ones = sb("ones", [P, P])
        sq = sb("sq", [P, T])
        ssum = sb("ssum", [P, T])
        ms = sb("ms", [P, T])
        rstd = sb("rstd", [P, T])
        tmp = sb("tmp", [P, T])
        e_pad = sb("e_pad", [P, 2, 2 + T])
        forget = sb("forget", [P, 2, T])
        mixed = sb("mixed", [P, PAIRS + HEADS, T])

        prob = w_raw[:, 0, UA:UA + 3 * P]
        prob_t = w_raw[:, 1, UA:UA + 3 * P]
        v_tok = w_raw[:, 2, UA:UA + 2 * P]
        row_stats = w_raw[:, 3, UA:UA + 4]
        row_max, row_sum = row_stats[:, 0:2], row_stats[:, 2:4]

        low = shared("low", [P, 4, T])
        lora_w = shared("lora_w", [P, 2, P])
        gate_w = shared("gate_w", [P, 2, P])
        qkv = shared("qkv", [P, 3, T])
        forget_sel = shared("forget_sel", [P, T])
        rkv = shared("rkv", [P, 3, T])
        gate = shared("gate", [P, T])
        iclr = shared("iclr", [P, T])
        log_w = shared("log_w", [P, T])
        kk = shared("kk", [P, T])
        kn = shared("kn", [P, T])
        rs = shared("rs", [P, T])
        cum = shared("cum", [P, 2, P + 1])
        neg_mid = shared("neg_mid", [P, 2])
        dec = shared("dec", [P, 2, P + 1])
        inv_dec = shared("inv_dec", [P, 2, P + 1])
        kr = shared("kr", [P, 2, 2 * P])
        kinv = shared("kinv", [P, 2, P])
        binv = shared("binv", [P, 2, P])
        tok = shared("tok", [P, 4, P])
        akr = shared("akr", [P, 4, 2 * P])
        abr = shared("abr", [P, 4, 2 * P])
        al = shared("al", [P, 4, P])
        inv = shared("inv", [P, 2, 4, P])
        off = shared("off", [P, 4, P])
        w1 = shared("w1", [P, 4, P])
        ru = shared("ru", [P, 2, P])
        state = shared("state", [P, P])
        state_scale = shared("state_scale", [P, 1])
        y = shared("y", [P, T])
        y_sq = shared("y_sq", [P, T])
        var = shared("var", [P, T])
        scope.close()
        h_next = sb("h_next", [P, DC, 2 * T], F32R)
        scope.close()
        u_t = sb("u_t", [P, 4, T])
        invc = sb("invc", [P, 4, T])
        win = sb("win", [P, 2, 16 + T])
        win_b = sb("win_b", [P, 2, 16 + T])
        sq_by = sb("sq_by", [P, 2, T])

        aux = ctx.enter_context(nc.psum_tensor("aux", [P, 6, 512], F32))
        acc = [ctx.enter_context(nc.psum_tensor(f"acc{b}", [P, 512], F32)) for b in range(2)] + [aux[:, 0], aux[:, 1]]

        params_landed = sem("params_landed")
        gain_landed = sem("gain_landed")
        x_landed = [sem(f"x_landed{q}") for q in range(4)]
        w_landed = [sem(f"w_landed{s}") for s in range(SLOTS)]
        names = {}

        def S(name):
            if name not in names:
                names[name] = sem(name)
            return names[name]

        hi_ready, lo_ready, units_done = S("hi_ready"), S("lo_ready"), S("units_done")
        acc_free = S("acc_free")
        x_done = S("x_chunks_final")

        def mat_b(k, n):
            return mat[:, k:k + 1, :].to_broadcast([P, n, P])

        block = ctx.enter_context(nc.Block())

        @block.sync
        def _(sp):
            sp.dma_start(gain[:], gains).then_inc(gain_landed, 16)
            for s in range(SLOTS):
                quarter = slice(4 * s, 4 * s + 4)
                sp.dma_start(x[:, quarter], x_in[:, quarter]).then_inc(x_landed[s], 16)
                sp.dma_start(w_raw[:, s, 0:UA], wa[s]).then_inc(w_landed[s], 16)
            for dst, src in ((mixp, mix_p), (mu_low, mu0), (bf, b_f), (mat, mats), (convp, conv_p),
                             (poolp, pool_p)):
                sp.dma_start(dst[:], src).then_inc(params_landed, 16)

            def load(w, first, g, n, cols):
                with sp.Fori(0, n) as i:
                    for s in range(SLOTS):
                        sp.wait_ge(lo_ready, 4 * i + (4 * g + s - 3))
                        src = w[bass.ds(4 * i + (4 * first + s), 1)].rearrange("o p c -> (o p) c")
                        sp.dma_start(w_raw[:, s, 0:cols], src).then_inc(w_landed[s], 16)

            load(wa, 1, 1, FIRST_FFN0 - 1, UA)
            sp.wait_ge(S("mixed_ready"), PAIRS + HEADS)
            sp.dma_start(invc[:], inv_count).then_inc(S("counts_landed"), 16)
            g, a, b = FIRST_FFN0, FIRST_FFN0, 0
            for layer in range(2):
                for q in range(QUARTERS):
                    load(wa, a, g, G_UP, UA)
                    load(wb, b, g + G_UP, G_DOWN, UB)
                    g, a, b = g + G_QUARTER, a + G_UP, b + G_DOWN
                if layer == 0:
                    load(wa, a, g, G_POOL, UA)
                    g, a = g + G_POOL, a + G_POOL
            for c in range(0, DC, 4):
                sp.wait_ge(S("out_ready"), c + 4)
                sp.dma_start(out[:, c:c + 4], x[:, c:c + 4]).then_inc(S("out_stored"), 16)
            sp.wait_ge(S("out_stored"), 16 * DC // 4)

        @block.gpsimd
        def _(pool):
            consts = S("consts_ready")
            for t, v in ((ones, 1.0), (e_pad, 0.0), (cum, 0.0), (akr, 0.0),
                         (abr, 0.0), (al, 0.0), (forget_sel, 0.0)):
                nc.gpsimd.memset(t[:], v).then_inc(consts, 1)
            pool.wait_ge(consts, N_CONSTS)

            def norm(n, k):
                if k:
                    pool.wait_ge(S("square_sum_ps"), n)
                nc.gpsimd.memset(ssum[:], 0.0).then_inc(S("sum_cleared"), 1)
                pool.wait_ge(S("sum_cleared"), k + 1)
                with pool.Fori(0, DC) as c:
                    pool.wait_ge(x_done, c + (DC * (n - 1) + 1))
                    nc.gpsimd.tensor_tensor(sq[:], chunk(x, c), chunk(x, c), ALU.mult).then_inc(S("squared"), 1)
                    pool.wait_ge(S("squared"), c + (DC * k + 1))
                    nc.gpsimd.tensor_tensor(ssum[:], ssum[:], sq[:], ALU.add).then_inc(S("summed"), 1)
                    pool.wait_ge(S("summed"), c + (DC * k + 1))

            for c in range(DC):
                if c % 4 == 0:
                    pool.wait_ge(x_landed[c // 4], 16)
                if c > 1:
                    pool.wait_ge(S("square_added"), c - 1)
                nc.gpsimd.tensor_tensor(sq_by[:, c % 2], x[:, c], x[:, c], ALU.mult).then_inc(S("squares_ready"), 1)

            with pool.Fori(0, PAIRS) as j:
                pool.wait_ge(S("al_masked"), 2 * j + 2)
                for lv in range(LEVELS):
                    if lv:
                        pool.wait_ge(S("w1_ps"), LEVELS * j + lv)
                    nc.gpsimd.tensor_tensor(off[:], al[:], mat_b(lv, 4), ALU.mult).then_inc(S("off_ready"), 1)
            norm(1, 0)
            norm(2, 1)
            own = Chain(pool, S("pool_own"))
            own.link(nc.gpsimd.memset(win_b[:, :, 0:16], 0.0))
            pool.wait_ge(S("pads_ready"), 1)
            pool.wait_ge(S("counts_landed"), 16)
            for c in range(DC // 2, DC):
                pool.wait_ge(acc_free, R_POOL + c - DC // 2 + 3)
                windows(nc.gpsimd, own, c, c // 4, win_b, pooled, invc)
                pool.sem_inc(S("pooled_ready"), 1)
            norm(4, 2)

        @block.scalar
        def _(act):
            def hi(g, s, cols):
                act.wait_ge(w_landed[s], 16 * g + 32)
                act.wait_ge(units_done, 4 * g + (s + 1))
                nc.scalar.activation(w_hi[:, s, 0:cols], w_raw[:, s, 0:cols], ACT.Identity).then_inc(hi_ready, 1)

            def tile(g, e, cols):
                hi(g, 2 * e, cols)
                hi(g, 2 * e + 1, cols)

            def root(n):
                act.wait_ge(S("mean_square_ready"), n + 1)
                nc.scalar.activation(ms[:], ms[:], ACT.Sqrt).then_inc(S("rms_ready"), 1)

            def next_h(which, c, n):
                act.wait_ge(x_done, n)
                nc.scalar.activation(chunk(h_next, c), chunk(x, c), ACT.Identity,
                                     scale=gain[:, which, bass.ds(c, 1)]).then_inc(S("h_hi_ready"), 1)

            def squares(c):
                if c:
                    act.wait_ge(S("square_added"), DC - 1 + c - 1)
                nc.scalar.activation(sq_by[:, c % 2], x[:, c], ACT.Square).then_inc(S("squares_ready"), 1)

            act.dma_start(lora_w[:], lora[0, :, 0:2]).then_inc(S("lora_landed"), 16)
            act.dma_start(gate_w[:], lora[0, :, 2:4]).then_inc(S("gate_landed"), 16)
            act.wait_ge(gain_landed, 16)
            for s in range(SLOTS):
                act.wait_ge(x_landed[s], 16)
                for c in range(4 * s, 4 * s + 4):
                    nc.scalar.activation(h[:, c, 0:T], x[:, c], ACT.Identity,
                                         scale=gain[:, 0, c:c + 1]).then_inc(S("h_hi_ready"), 1)
                act.wait_ge(w_landed[s], 16)
                nc.scalar.activation(w_hi[:, s, 0:UA], w_raw[:, s, 0:UA], ACT.Identity).then_inc(hi_ready, 1)
            act.wait_ge(params_landed, 16 * N_PARAMS)
            root(0)
            for g in range(G_LOW):
                for e in range(2):
                    tile(g, e, UA)
            act.wait_ge(S("low_shifted"), 1)
            nc.scalar.activation(low[0:LORA, 1], low[0:LORA, 1], ACT.Tanh).then_inc(S("low_tanh"), 1)
            nc.scalar.activation(low[:, 2:4], low[:, 2:4], ACT.Tanh, scale=0.5).then_inc(S("low_tanh"), 1)
            act.wait_ge(S("forget_abs"), 1)
            fg = forget[LORA:LORA + HEADS, 1]
            nc.scalar.activation(fg, fg, ACT.Exp, scale=-1.0).then_inc(S("forget_exp"), 1)
            act.wait_ge(S("forget_exp"), 1)
            nc.scalar.activation(fg, fg, ACT.Ln, bias=ones[LORA:LORA + HEADS, 0:1]).then_inc(S("forget_ln"), 1)

            def unit_hi(i, u):
                hi(TILES // 2 * i + (FIRST_IN + u // SLOTS), u % SLOTS, UA)

            def low_rank(i):
                par = lambda k: mixp[:, bass.ds(i, 1), k]
                act.wait_ge(S("lora_ps"), i + 1)
                act.dma_start(lora_w[:], lora[bass.ds(i + 1, 1), :, 0:2].rearrange("o p a b -> (o p) a b")) \
                    .then_inc(S("lora_landed"), 16)
                nc.scalar.activation(iclr[:], aux[:, 4, 0:T], ACT.Tanh, scale=0.5, bias=par(A0))
                nc.scalar.activation(log_w[:], aux[:, 4, T:2 * T], ACT.Tanh, scale=0.5, bias=par(W0)) \
                    .then_inc(S("lora_read"), 1)

            def decays(i):
                act.wait_ge(S("cum_ready"), i + 1)
                for c in range(2):
                    nc.scalar.activation(dec[:, c], cum[:, c], ACT.Exp, bias=neg_mid[:, c:c + 1])
                for c in range(2):
                    ins = nc.scalar.activation(inv_dec[:, c], cum[:, c], ACT.Exp, scale=-1.0,
                                               bias=cum[:, c, P // 2:P // 2 + 1])
                ins.then_inc(S("decay_ready"), 1)

            def copy_w1(j, lv):
                act.wait_ge(S("w1_ps"), LEVELS * j + (lv + 1))
                nc.scalar.activation(w1[:], aux[:, 0].rearrange("p (a b) -> p a b", a=4), ACT.Identity) \
                    .then_inc(S("w1_ready"), 1)

            def copy_ru(j, k):
                act.wait_ge(S("ru_ps"), 4 * j + (k + 1))
                nc.scalar.activation(ru[:, k % 2], aux[:, 0, 0:P], ACT.Identity).then_inc(S("ru_ready"), 1)

            def out_hi(*units):
                for u in units:
                    hi(FIRST_OUT + u // SLOTS, u % SLOTS, UA)

            def mixed_hi(*places):
                for k in places:
                    nc.scalar.activation(h[:, k, 0:T], mixed[:, MIX_ORDER[k]], ACT.Identity) \
                        .then_inc(S("mixed_hi_ready"), 1)

            def body(i, mix, load):
                j, out_too = i - 1, not load
                par = lambda k: mixp[:, bass.ds(j, 1), k]
                if load:
                    unit_hi(i, 0)
                    unit_hi(i, 1)
                if out_too:
                    act.wait_ge(units_done, 4 * FIRST_OUT)
                    act.wait_ge(S("rwkv_done"), PAIRS - 1)
                    act.wait_ge(S("attn_done"), HEADS - 1)
                    mixed_hi(*range(14))
                    out_hi(0, 1, 2)
                if mix:
                    copy_w1(j, 0)
                if load:
                    unit_hi(i, 2)
                if mix:
                    if out_too:
                        out_hi(3)
                    copy_w1(j, 1)
                    if out_too:
                        out_hi(4)
                if load:
                    unit_hi(i, 3)
                if mix:
                    act.wait_ge(S("scores_ready"), j + 1)
                    nc.scalar.activation(prob[:, 0:P], prob[:, 0:P], ACT.Exp, scale=ATT_SCALE, bias=row_max[:, 0:1],
                                         accum_out=row_sum[:, 0:1])
                    nc.scalar.activation(prob[:, P:3 * P], prob[:, P:3 * P], ACT.Exp, scale=ATT_SCALE,
                                         bias=row_max[:, 1:2], accum_out=row_sum[:, 1:2]).then_inc(S("exp_ready"), 1)
                    copy_w1(j, 2)
                    if out_too:
                        out_hi(5)
                if load:
                    unit_hi(i, 4)
                if mix:
                    act.wait_ge(S("fox_turned_ps"), j + 1)
                    nc.scalar.activation(prob_t, aux[:, 4, 0:3 * P], ACT.Identity)
                    nc.scalar.activation(v_tok, aux[:, 5, 0:T], ACT.Identity).then_inc(S("fox_turned"), 1)
                    copy_w1(j, 3)
                    if out_too:
                        out_hi(6, 7)
                if load:
                    unit_hi(i, 5)
                if mix:
                    copy_w1(j, 4)
                    if out_too:
                        act.wait_ge(S("attn_done"), HEADS)
                        mixed_hi(14)
                        out_hi(8)
                if load:
                    low_rank(i)
                    unit_hi(i, 6)
                if mix:
                    copy_w1(j, 5)
                    if out_too:
                        out_hi(9)
                    copy_ru(j, 0)
                    if out_too:
                        out_hi(10)
                if load:
                    decays(i)
                if mix:
                    copy_ru(j, 1)
                    if out_too:
                        out_hi(11)
                if load:
                    unit_hi(i, 7)
                    act.wait_ge(S("key_norm_ready"), i + 1)
                    nc.scalar.activation(rs[:], rs[:], ACT.Sqrt).then_inc(S("key_root_ready"), 1)
                    unit_hi(i, 8)
                if mix:
                    copy_ru(j, 2)
                if mix:
                    copy_ru(j, 3)
                    if out_too:
                        out_hi(12)
                if load:
                    unit_hi(i, 9)
                if mix:
                    act.wait_ge(S("y_ps"), j + 1)
                    nc.scalar.activation(y[:], aux[:, 3, 0:T], ACT.Identity).then_inc(S("y_ready"), 1)
                    if out_too:
                        out_hi(13)
                    act.wait_ge(S("gate_ps"), j + 1)
                    act.dma_start(gate_w[:], lora[bass.ds(j + 1, 1), :, 2:4].rearrange("o p a b -> (o p) a b")) \
                        .then_inc(S("gate_landed"), 16)
                    nc.scalar.activation(gate[:], aux[:, 3, 0:T], ACT.Identity).then_inc(S("gate_read"), 1)
                    act.wait_ge(S("y_centred"), j + 1)
                    nc.scalar.activation(y_sq[:], y[:], ACT.Square).then_inc(S("y_squared"), 1)
                    if out_too:
                        out_hi(14)
                if load:
                    unit_hi(i, 10)
                    act.wait_ge(S("turned_ps"), i + 1)
                    nc.scalar.activation(tok[:], aux[:, 4].rearrange("p (a b) -> p a b", a=4), ACT.Identity) \
                        .then_inc(S("tok_ready"), 1)
                if mix:
                    act.wait_ge(S("var_ready"), j + 1)
                    nc.scalar.activation(var[:], var[:], ACT.Sqrt).then_inc(S("group_root_ready"), 1)
                if load:
                    unit_hi(i, 11)
                if mix:
                    act.wait_ge(S("y_scaled"), j + 1)
                    nc.scalar.activation(y[:], y[:], ACT.Identity, scale=par(GN_W), bias=par(GN_B)) \
                        .then_inc(S("group_norm_ready"), 1)

            act.wait_ge(S("halved"), 1)
            body(0, False, True)
            with act.Fori(1, PAIRS) as i:
                body(i, True, True)
            body(PAIRS, True, False)

            act.wait_ge(S("rwkv_done"), PAIRS)
            act.wait_ge(S("attn_done"), HEADS)
            act.wait_ge(S("lora_landed"), 16 * (PAIRS + 1))
            act.wait_ge(S("gate_landed"), 16 * (PAIRS + 1))
            mixed_hi(15)
            out_hi(15)

            with act.Fori(0, G_OUT // 2) as i:
                for s in range(SLOTS):
                    hi(i + SECOND_OUT, s, UA)
                    next_h(2, 4 * i + s, 4 * i + (s + 1))

            def feature_hi(pair, c):
                act.wait_ge(S("product_ready"), pair + 1)
                nc.scalar.activation(chunk(h, c), u_t[:, 3], ACT.Identity).then_inc(S("feature_hi_ready"), 1)

            def tap(n, conv, e):
                act.wait_ge(acc_free, n + e + 3)
                par = lambda k: convp[:, bass.ds(conv + e, 1), k]
                nc.scalar.activation(u_t[:, e], e_pad[:, e, 2:], ACT.Identity, scale=par(2), bias=par(3)) \
                    .then_inc(S("tap_ready"), 1)

            def up_pair(g, n, pair, c, conv, cols, first=False, last=False):
                hi(g, 0, cols)
                if not first:
                    feature_hi(pair - 1, c - 1)
                hi(g, 1, cols)
                tap(n, conv, 0)
                hi(g, 2, cols)
                act.wait_ge(S("gate_ready"), pair + 1)
                nc.scalar.activation(u_t[:, 2], u_t[:, 0], ACT.Tanh, scale=0.5).then_inc(S("tanh_ready"), 1)
                if not last:
                    hi(g, 3, cols)
                tap(n, conv, 1)
                if last:
                    feature_hi(pair, c)
                    hi(g, 3, cols)

            for layer in range(2):
                g0, n0, p0 = FIRST_FFN[layer], R_FFN[layer], layer * QUARTERS * G_UP
                for q in range(QUARTERS):
                    if q == 0:
                        root(1 + 2 * layer)
                    up_pair(g0, n0, p0, 0, 2 * p0, UA, first=True)
                    with act.Fori(1, G_UP - 1) as i:
                        up_pair(i + g0, 2 * i + n0, i + p0, i, 2 * i + 2 * p0, UA)
                    last = G_UP - 1
                    up_pair(g0 + last, n0 + 2 * last, p0 + last, last, 2 * (p0 + last), UB, last=True)
                    to_pool = layer == 0 and q == QUARTERS - 1

                    def down_unit(i, s, cols):
                        if cols:
                            hi(i + (g0 + G_UP), s, cols)
                        if to_pool:
                            next_h(1, 4 * i + s, 4 * i + (DC + s + 1))

                    with act.Fori(0, G_DOWN - 1) as i:
                        for s in range(SLOTS):
                            down_unit(i, s, UB)
                    for s in range(SLOTS):
                        down_unit(G_DOWN - 1, s, None if layer == 1 and q == QUARTERS - 1 else UA)
                    g0, n0, p0 = g0 + G_QUARTER, n0 + R_QUARTER, p0 + G_UP
                if layer == 0:
                    hi(FIRST_POOL, 0, UA)
                    root(2)
                    for u in range(1, 4 * G_POOL):
                        hi(FIRST_POOL + u // 4, u % 4, UA)
                    for c in range(DC):
                        next_h(3, c, 2 * DC + c + 1)
                        squares(c)
            root(4)

        @block.vector
        def _(dve):
            own = Chain(dve, S("dve_own"))
            tt, ts, stt = nc.vector.tensor_tensor, nc.vector.tensor_scalar, nc.vector.scalar_tensor_tensor
            dve.sem_inc(acc_free, 2)

            def lo(g, s, cols):
                dve.wait_ge(hi_ready, 4 * g + (s + 5))
                tt(w_lo[:, s, 0:cols], w_raw[:, s, 0:cols], w_hi[:, s, 0:cols].bitcast(F32), ALU.subtract) \
                    .then_inc(lo_ready, 1)

            def read_result(bank, n, done, read):
                dve.wait_ge(units_done, done)
                read(acc[bank][:, 0:T]).then_inc(acc_free, 1)
                dve.wait_ge(acc_free, n + 3)

            def times_rstd(dst):
                return lambda result: tt(dst, result, rstd[:], ALU.mult)

            def scaled_result(b, bank, n):
                read_result(bank, n, 2 * n + 2, times_rstd(e_pad[:, b, 2:]))

            def shifted(dst, b, mu, rows=P):
                e, before = e_pad[0:rows, b, 2:], e_pad[0:rows, b, 1:1 + T]
                own.link(tt(tmp[0:rows], before, e, ALU.subtract))
                return stt(out=dst, in0=tmp[0:rows], scalar=mu, in1=e, op0=ALU.mult, op1=ALU.add)

            def split(dst, c, src):
                own.link(nc.vector.tensor_copy(chunk(dst, c), src))
                return tt(chunk(dst, c, T, 2 * T), src, chunk(dst, c).bitcast(F32), ALU.subtract)

            def next_h(which, c, n, h=h_next):
                dve.wait_ge(S("h_hi_ready"), n)
                stt(out=chunk(h, c, T, 2 * T), in0=chunk(x, c), scalar=gain[:, which, bass.ds(c, 1)],
                    in1=chunk(h, c).bitcast(F32), op0=ALU.mult, op1=ALU.subtract).then_inc(S("h_ready"), 1)

            def mean_square(n):
                dve.wait_ge(S("square_sum_ps"), n + 1)
                ts(ms[:], aux[:, 4, 0:T], 1.0 / D, RMS_EPS, ALU.mult, ALU.add).then_inc(S("mean_square_ready"), 1)
                dve.wait_ge(S("rms_ready"), n + 1)
                nc.vector.reciprocal(rstd[:], ms[:]).then_inc(S("rstd_ready"), 1)
                dve.wait_ge(S("rstd_ready"), n + 1)

            dve.wait_ge(gain_landed, 16)
            for s in range(SLOTS):
                dve.wait_ge(x_landed[s], 16)
                for c in range(4 * s, 4 * s + 4):
                    next_h(0, c, c + 1, h)
                lo(-1, s, UA)
            dve.wait_ge(params_landed, 16 * N_PARAMS)
            dve.wait_ge(S("consts_ready"), N_CONSTS)
            for c in range(2):
                own.link(nc.vector.tensor_copy(mask[:, c].rearrange("p (a b) -> p a b", a=3), mat[:, MASKS:MASKS + 3]))
            ts(mixp[:, :, W0:A0 + 1], mixp[:, :, W0:A0 + 1], 0.5, None, ALU.mult).then_inc(S("halved"), 1)
            mean_square(0)
            for g in range(G_LOW):
                for e in range(2):
                    n = 2 * g + e
                    lo(g, 2 * e, UA)
                    scaled_result(e, n % 2, n)
                    lo(g, 2 * e + 1, UA)
                    if n == 0:
                        rows = slice(LORA, LORA + HEADS)
                        fx, fm = forget[rows, 0], forget[rows, 1]
                        own.link(ts(fx, e_pad[rows, 0, 2:], bf[rows, 0:1], None, ALU.add))
                        stt(out=fm, in0=fx, scalar=-1.0, in1=fx, op0=ALU.mult, op1=ALU.max) \
                            .then_inc(S("forget_abs"), 1)
                    rows = LORA if n < 2 else P
                    ins = shifted(low[0:rows, n], e, mu_low[0:rows, n:n + 1], rows)
                    if n < 3:
                        own.link(ins)
                    else:
                        ins.then_inc(S("low_shifted"), 1)
            dve.wait_ge(S("low_tanh"), 2)
            ts(low[:, 2:4], low[:, 2:4], 0.5, 0.5, ALU.mult, ALU.add).then_inc(S("low_ready"), 1)
            dve.wait_ge(S("forget_ln"), 1)
            rows = slice(LORA, LORA + HEADS)
            own.link(stt(out=forget[rows, 0], in0=forget[rows, 0], scalar=0.0, in1=forget[rows, 1], op0=ALU.min,
                         op1=ALU.subtract))
            own.link(nc.vector.tensor_tensor_scan(forget[rows, 1], ones[rows, 0:1].to_broadcast([HEADS, T]), forget[rows, 0], 0.0, ALU.mult,
                                                  ALU.add))
            ts(forget[rows, 0], forget[rows, 1], -1.0 / ATT_SCALE, None, ALU.mult).then_inc(S("forget_ready"), 1)

            def unit_lo(i, u):
                lo(TILES // 2 * i + (FIRST_IN + u // SLOTS), u % SLOTS, UA)

            def rwkv_result(i, t):
                scaled_result(t % 2, t % 2, TILES * i + (2 * FIRST_IN + t))
                own.link(shifted(rkv[:, t], t % 2, mixp[:, bass.ds(i, 1), MU_R + t]))

            def fox_result(i, t):
                n = TILES * i + (2 * FIRST_IN + t)
                read_result(t % 2, n, 2 * n + 2, times_rstd(qkv[:, t - 3]))

            r, k, v = rkv[:, 0], rkv[:, 1], rkv[:, 2]
            halves = lambda t: t.rearrange("p (a b) -> p a b", a=2)

            def key_square(i):
                own.link(ts(kk[:], k, mixp[:, bass.ds(i, 1), K_K], None, ALU.mult))
                tt(kn[:], kk[:], kk[:], ALU.mult).then_inc(S("key_squared"), 1)

            def key_norm(i):
                dve.wait_ge(S("key_norm_ps"), i + 1)
                ts(rs[:], aux[:, 5, 0:T], 1e-24, None, ALU.max).then_inc(S("key_norm_ready"), 1)

            def low_rank(i):
                dve.wait_ge(S("lora_read"), i + 1)
                own.link(ts(log_w[:], log_w[:], -EXP_HALF / 2, -EXP_HALF / 2, ALU.mult, ALU.add))
                a = own.mark(ts(iclr[:], iclr[:], 0.5, 0.5, ALU.mult, ALU.add))
                for c in range(2):
                    scan = own.mark(nc.vector.tensor_tensor_scan(cum[:, c, 1:], ones[:], log_w[:, c * P:c * P + P],
                                                                 0.0, ALU.mult, ALU.add))
                own.done(scan)
                ts(neg_mid[:], cum[:, :, P // 2], -1.0, None, ALU.mult).then_inc(S("cum_ready"), 1)

            def bonus_product(i):
                own.link(ts(y[:], iclr[:], 1.0, mixp[:, bass.ds(i, 1), K_A], ALU.subtract, ALU.mult))
                own.link(stt(out=k, in0=y[:], scalar=1.0, in1=k, op0=ALU.add, op1=ALU.mult))
                stt(out=y_sq[:], in0=r, scalar=mixp[:, bass.ds(i, 1), R_K], in1=k, op0=ALU.mult, op1=ALU.mult) \
                    .then_inc(S("bonus_product"), 1)

            def bonus(i):
                dve.wait_ge(S("bonus_ps"), i + 1)
                tt(chunk(mixed, i), aux[:, 1, 0:T], v, ALU.mult).then_inc(S("bonus_ready"), 1)

            def keys(i):
                dve.wait_ge(S("key_root_ready"), i + 1)
                own.link(nc.vector.reciprocal(rs[:], rs[:]))
                own.link(tt(kk[:], kk[:], rs[:], ALU.mult))
                own.link(stt(out=kn[:], in0=kk[:], scalar=-1.0, in1=iclr[:], op0=ALU.mult, op1=ALU.mult))
                dve.wait_ge(S("decay_ready"), i + 1)
                tt(kinv[:], halves(k), inv_dec[:, :, 1:], ALU.mult)
                tt(binv[:], halves(kn[:]), inv_dec[:, :, 1:], ALU.mult).then_inc(S("keys_ready"), 1)

            def queries(i):
                tt(kr[:, :, 0:P], halves(kk[:]), dec[:, :, 0:P], ALU.mult)
                tt(kr[:, :, P:2 * P], halves(r), dec[:, :, 1:], ALU.mult).then_inc(S("queries_ready"), 1)

            def masked_grams(j):
                dve.wait_ge(S("grams_ps"), 2 * j + 2)
                tt(state_scale[:], dec[:, 0, P:P + 1], inv_dec[:, 1, 0:1], ALU.mult)
                for hd in range(2):
                    nc.vector.copy_predicated(al[:, 2 * hd:2 * hd + 2], mask[:, :, 2 * P:],
                                              aux[:, 4 + hd, 0:2 * P].rearrange("p (a b) -> p a b", a=2)) \
                        .then_inc(S("al_masked"), 1)
                for hd in range(2):
                    nc.vector.copy_predicated(abr[:, 2 * hd:2 * hd + 2], mask[:, :, 0:2 * P],
                                              aux[:, 2 + hd].rearrange("p (a b) -> p a b", a=2)) \
                        .then_inc(S("abr_masked"), 1)
                dve.wait_ge(S("al_masked"), 2 * j + 2)
                low_blocks = own.mark(tt(inv[:, 1], al[:], mat_b(ONE_LOW, 4), ALU.mult))
                dve.wait_ge(S("abr_masked"), 2 * j + 2)
                up_blocks = own.mark(tt(inv[:, 0], abr[:, :, 0:P], mat_b(ONE_UP, 4), ALU.mult))
                own.done(low_blocks)
                tt(inv[:, 1], inv[:, 1], mat_b(IDENT, 4), ALU.add).then_inc(S("inv_ready"), 1)
                own.done(up_blocks)
                tt(inv[:, 0], inv[:, 0], mat_b(IDENT, 4), ALU.add).then_inc(S("inv_t_ready"), 1)
                for hd in range(2):
                    nc.vector.copy_predicated(akr[:, 2 * hd:2 * hd + 2], mask[:, :, 0:2 * P],
                                              aux[:, hd].rearrange("p (a b) -> p a b", a=2)) \
                        .then_inc(S("akr_masked"), 1)

            def doubled(j, lv):
                def add(m, bank):
                    n = P >> (lv + 2)
                    blocks = half_blocks(inv[:, m].rearrange("p a b -> p (a b)"), lv, 1 - m)
                    return tt(blocks, blocks, aux[:, bank, 0:2 * P].rearrange("p (n b) -> p n b", n=4 * n), ALU.add)
                dve.wait_ge(S("inv_t_ps"), LEVELS * j + (lv + 1))
                dve.wait_ge(S("inv_t_ready"), (LEVELS + 1) * j + (lv + 1))
                add(0, 2).then_inc(S("inv_t_ready"), 1)
                if lv < LEVELS - 1:
                    dve.wait_ge(S("inv_ps"), (LEVELS - 1) * j + (lv + 1))
                    dve.wait_ge(S("inv_ready"), LEVELS * j + (lv + 1))
                    add(1, 3).then_inc(S("inv_ready"), 1)

            def next_state(j):
                dve.wait_ge(S("state_ps"), j + 1)
                stt(out=state[:], in0=aux[:, 2, 0:P], scalar=state_scale[:], in1=mat[:, HEAD_BLOCKS], op0=ALU.mult,
                    op1=ALU.mult).then_inc(S("state_ready"), 1)

            def centred(j):
                dve.wait_ge(S("mean_ps"), j + 1)
                stt(out=y[:], in0=aux[:, 2, 0:T], scalar=-1.0 / 64, in1=y[:], op0=ALU.mult, op1=ALU.add) \
                    .then_inc(S("y_centred"), 1)

            def variance(j):
                dve.wait_ge(S("var_ps"), j + 1)
                ts(var[:], aux[:, 0, 0:T], 1.0 / 64, GN_EPS, ALU.mult, ALU.add).then_inc(S("var_ready"), 1)

            def normed(j):
                dve.wait_ge(S("group_root_ready"), j + 1)
                own.link(nc.vector.reciprocal(var[:], var[:]))
                tt(y[:], y[:], var[:], ALU.mult).then_inc(S("y_scaled"), 1)

            def gated(j):
                dve.wait_ge(S("group_norm_ready"), j + 1)
                own.link(tt(y[:], y[:], chunk(mixed, j), ALU.add))
                dve.wait_ge(S("gate_read"), j + 1)
                tt(chunk(mixed, j), y[:], gate[:], ALU.mult).then_inc(S("rwkv_done"), 1)

            def scores(n):
                dve.wait_ge(S("scores_ps"), n + 1)
                first = own.mark(tt(prob[:, 0:P], aux[:, 1, 0:P], mat[:, CAUSAL], ALU.add))
                own.mark(nc.vector.tensor_copy(prob[:, P:2 * P], aux[:, 1, P:2 * P]))
                second = own.mark(tt(prob[:, 2 * P:], aux[:, 1, 2 * P:3 * P], mat[:, CAUSAL], ALU.add))
                own.done(first)
                own.mark(nc.vector.tensor_reduce(row_max[:, 0:1], prob[:, 0:P], AX.X, ALU.max))
                own.done(second)
                own.link(nc.vector.tensor_reduce(row_max[:, 1:2], prob[:, P:], AX.X, ALU.max))
                ts(row_max, row_max, -ATT_SCALE, None, ALU.mult).then_inc(S("scores_ready"), 1)

            def probabilities(n):
                dve.wait_ge(S("exp_ready"), n + 1)
                own.link(nc.vector.reciprocal(row_sum, row_sum))
                ts(prob[:, 0:P], prob[:, 0:P], row_sum[:, 0:1], None, ALU.mult)
                ts(prob[:, P:], prob[:, P:], row_sum[:, 1:2], None, ALU.mult).then_inc(S("probs_ready"), 1)

            def attended(n):
                dve.wait_ge(S("attn_ps"), n + 1)
                nc.vector.tensor_copy(chunk(mixed, n + PAIRS), aux[:, 1, 0:T]).then_inc(S("attn_done"), 1)

            def add_to_x(c, bank, n, done, final):
                dve.wait_ge(units_done, done)
                ins = tt(chunk(x, c), chunk(x, c), acc[bank][:, 0:T], ALU.add)
                if final is None:
                    ins.then_inc(acc_free, 1)
                else:
                    ins.then_inc(x_done, 1)
                    dve.wait_ge(x_done, final)
                    dve.sem_inc(acc_free, 1)

            def out_unit(*units):
                for u in units:
                    add_to_x(u, u % 2, R_OUT + u, 4 * FIRST_OUT + u + 1, None)
                    lo(FIRST_OUT + u // SLOTS, u % SLOTS, UA)

            def mixed_lo(*places):
                for k in places:
                    dve.wait_ge(S("mixed_hi_ready"), k + 1)
                    tt(h[:, k, T:2 * T], mixed[:, MIX_ORDER[k]], h[:, k, 0:T].bitcast(F32), ALU.subtract) \
                        .then_inc(S("mixed_ready"), 1)

            def body(i, mix, load):
                j, out_too = i - 1, not load
                if out_too:
                    mixed_lo(*range(8))
                if mix:
                    masked_grams(j)
                if out_too:
                    out_unit(0, 1, 2)
                if load:
                    unit_lo(i, 0)
                    rwkv_result(i, 0)
                    unit_lo(i, 1)
                if mix:
                    doubled(j, 0)
                    if out_too:
                        out_unit(3)
                if load:
                    unit_lo(i, 2)
                if mix:
                    scores(j)
                    doubled(j, 1)
                    if out_too:
                        out_unit(4)
                if load:
                    rwkv_result(i, 1)
                    unit_lo(i, 3)
                if mix:
                    probabilities(j)
                    doubled(j, 2)
                    if out_too:
                        mixed_lo(*range(8, 14))
                        out_unit(5)
                if load:
                    unit_lo(i, 4)
                if mix:
                    doubled(j, 3)
                    if out_too:
                        out_unit(6)
                    attended(j)
                    if out_too:
                        out_unit(7)
                if load:
                    rwkv_result(i, 2)
                    key_square(i)
                    unit_lo(i, 5)
                if mix:
                    doubled(j, 4)
                    if out_too:
                        out_unit(8)
                        mixed_lo(14)
                if load:
                    low_rank(i)
                    unit_lo(i, 6)
                if mix:
                    doubled(j, 5)
                    if out_too:
                        out_unit(9, 10)
                if load:
                    key_norm(i)
                    fox_result(i, 3)
                    bonus_product(i)
                    unit_lo(i, 7)
                if mix:
                    next_state(j)
                    if out_too:
                        out_unit(11, 12, 13)
                if load:
                    unit_lo(i, 8)
                    bonus(i)
                    fox_result(i, 4)
                    keys(i)
                    unit_lo(i, 9)
                if mix:
                    centred(j)
                if load:
                    queries(i)
                    unit_lo(i, 10)
                if mix:
                    variance(j)
                    if out_too:
                        out_unit(14)
                if load:
                    fox_result(i, 5)
                    rows = slice(LORA, LORA + HEADS)
                    ts(forget_sel[rows], forget[rows, 0], mat[rows, IDENT, bass.ds(i + LORA, 1)], None, ALU.mult) \
                        .then_inc(S("qkv_ready"), 1)
                if mix:
                    normed(j)
                if load:
                    unit_lo(i, 11)
                if mix:
                    gated(j)

            body(0, False, True)
            with own.loop(PAIRS, 26, start=1) as i:
                body(i, True, True)
            body(PAIRS, True, False)

            mixed_lo(15)
            out_unit(15)
            with own.loop(G_OUT // 2, 0) as i:
                for s in range(SLOTS):
                    add_to_x(4 * i + s, s % 2, 4 * i + (R_OUT + DC + s), 4 * i + (4 * SECOND_OUT + s + 1),
                             4 * i + (s + 1))
                    lo(i + SECOND_OUT, s, UA)
                    next_h(2, 4 * i + s, 4 * i + (DC + s + 1))
            mean_square(1)

            def taps(conv, e, k):
                return stt(out=u_t[:, e], in0=e_pad[:, e, k:k + T], scalar=convp[:, bass.ds(conv + e, 1), k],
                           in1=u_t[:, e], op0=ALU.mult, op1=ALU.add)

            def scaled(g, e, n):
                read_result(e, n, 4 * g + (2 * e + 2), times_rstd(e_pad[:, e, 2:]))

            def up_pair(g, n, pair, c, conv, cols, first=False, last=False):
                if not first:
                    rest_taps(pair - 1, conv - 2)
                lo(g, 0, cols)
                if not first:
                    rest_product(pair - 1)
                scaled(g, 0, n)
                if not first:
                    rest_lo(pair - 1, c - 1)
                lo(g, 1, cols)
                dve.wait_ge(S("tap_ready"), 2 * pair + 1)
                own.link(taps(conv, 0, 1))
                taps(conv, 0, 0).then_inc(S("gate_ready"), 1)
                lo(g, 2, cols)
                scaled(g, 1, n + 1)
                if last:
                    rest_taps(pair, conv)
                    rest_product(pair)
                    rest_lo(pair, c)
                lo(g, 3, cols)

            def rest_taps(pair, conv):
                dve.wait_ge(S("tap_ready"), 2 * pair + 2)
                t = own.mark(taps(conv, 1, 1))
                dve.wait_ge(S("tanh_ready"), pair + 1)
                own.mark(stt(out=u_t[:, 2], in0=u_t[:, 2], scalar=1.0, in1=u_t[:, 0], op0=ALU.add, op1=ALU.mult))
                own.done(t)
                own.value = own.mark(taps(conv, 1, 0))

            def rest_product(pair):
                own.done(own.value)
                stt(out=u_t[:, 3], in0=u_t[:, 2], scalar=0.5, in1=u_t[:, 1], op0=ALU.mult, op1=ALU.mult) \
                    .then_inc(S("product_ready"), 1)

            def rest_lo(pair, c):
                dve.wait_ge(S("feature_hi_ready"), pair + 1)
                tt(chunk(h, c, T, 2 * T), u_t[:, 3], chunk(h, c).bitcast(F32), ALU.subtract) \
                    .then_inc(S("features_ready"), 1)

            for layer in range(2):
                dve.wait_ge(S("rstd_ready"), 2 + 2 * layer)
                g0, n0, p0 = FIRST_FFN[layer], R_FFN[layer], layer * QUARTERS * G_UP
                for q in range(QUARTERS):
                    final = q == QUARTERS - 1
                    last = G_UP - 1
                    up_pair(g0, n0, p0, 0, 2 * p0, UA, first=True)
                    with own.loop(last, 4, start=1) as i:
                        up_pair(i + g0, 2 * i + n0, i + p0, i, 2 * i + 2 * p0, UA)
                    up_pair(g0 + last, n0 + 2 * last, p0 + last, last, 2 * (p0 + last), UB, last=True)
                    g1, n1 = g0 + G_UP, n0 + 2 * G_UP

                    def down_group(i, cols):
                        for s in range(SLOTS):
                            add_to_x(4 * i + s, s % 2, 4 * i + (n1 + s), 4 * i + (4 * g1 + s + 1),
                                     4 * i + (DC * (1 + 2 * layer) + s + 1) if final else None)
                            if cols:
                                lo(i + g1, s, cols)
                            if final and layer == 0:
                                next_h(1, 4 * i + s, 4 * i + (2 * DC + s + 1))

                    with dve.Fori(0, G_DOWN - 1) as i:
                        down_group(i, UB)
                    down_group(G_DOWN - 1, None if final and layer == 1 else UA)
                    g0, n0, p0 = g0 + G_QUARTER, n0 + R_QUARTER, p0 + G_UP
                mean_square(2 + 2 * layer)
                if layer == 0:
                    def prepared(c):
                        next_h(3, c, 3 * DC + c + 1)

                    zero = own.mark(nc.vector.memset(win[:, :, 0:16], 0.0))
                    nc.vector.memset(pooled[:, :, 0:16], 0.0).then_inc(S("pads_ready"), 1)
                    own.done(zero)
                    dve.wait_ge(S("counts_landed"), 16)
                    for u, first in enumerate(POOL_CHUNKS):
                        for r in range(2):
                            read_result(2 * (u % 2) + r, R_POOL + 2 * u + r, 4 * FIRST_POOL + u + 1,
                                        times_rstd(pooled[:, first + r, 16:]))
                        lo(FIRST_POOL + u // 4, u % 4, UA)
                    for c in range(DC):
                        if c < DC // 2:
                            windows(nc.vector, own, c, c // 4, win, pooled, invc)
                        else:
                            dve.wait_ge(S("pooled_ready"), c - DC // 2 + 1)
                        stt(out=x[:, c], in0=pooled[:, c, 16:], scalar=poolp[:, c:c + 1], in1=x[:, c],
                            op0=ALU.mult, op1=ALU.add).then_inc(x_done, 1)
                        if c:
                            prepared(c - 1)
                    prepared(DC - 1)
                    mean_square(3)
            dve.wait_ge(S("rstd_ready"), 5)
            for c in range(DC):
                stt(out=x[:, c], in0=x[:, c], scalar=gain[:, 4, c:c + 1], in1=rstd[:], op0=ALU.mult,
                    op1=ALU.mult).then_inc(S("out_ready"), 1)

        @block.tensor
        def _(pe):
            mm = nc.tensor.matmul

            def block_product(bank, s, b, rhs, start, stop):
                cols = slice(b * P, b * P + P)
                mm(acc[bank][:, 0:T], w_hi[:, s, cols], rhs[:, 0:T], start=start, stop=False, skip_group_check=True)
                mm(acc[bank][:, 0:T], w_hi[:, s, cols], rhs[:, T:2 * T], start=False, stop=False,
                   skip_group_check=True)
                return mm(acc[bank][:, 0:T], w_lo[:, s, cols], rhs[:, 0:T], start=False, stop=stop,
                          skip_group_check=True)

            def tile(g, e, bank, n, src, ready, count, between=None, each=None):
                pe.wait_ge(acc_free, n + 1)
                for half in range(2):
                    s = 2 * e + half
                    pe.wait_ge(lo_ready, 4 * g + (s + 1))
                    if each is None:
                        pe.wait_ge(ready, count - (8 if half == 0 else 1))
                    for b in range(8):
                        c = 8 * half + b
                        if c == DC - 1 or each is not None:
                            pe.wait_ge(ready, count - (DC - 1 - c))
                        ins = block_product(bank, s, b, src[:, c], c == 0, c == DC - 1)
                        if b == 7:
                            ins.then_inc(units_done, 1)
                        if each is not None:
                            each(c)
                    if half == 0 and between is not None:
                        square_sum(*between)

            def square_sum(n, k):
                pe.wait_ge(S("summed"), DC * (k + 1))
                mm(aux[:, 4, 0:T], ones[:], ssum[:], start=True, stop=True).then_inc(S("square_sum_ps"), 1)

            def add_square(k):
                pe.wait_ge(S("squares_ready"), k + 1)
                ins = mm(aux[:, 4, 0:T], ones[:], sq_by[:, k % 2], start=k % DC == 0, stop=k % DC == DC - 1,
                         skip_group_check=True)
                ins.then_inc(S("square_added") if k % DC < DC - 1 else S("square_sum_ps"), 1)

            pe.wait_ge(S("consts_ready"), N_CONSTS)
            for g in range(G_LOW):
                for e in range(2):
                    tile(g, e, e, 2 * g + e, h, S("h_ready"), DC, each=add_square if g == e == 0 else None)

            heads = [slice(64 * hd, 64 * hd + 64) for hd in range(2)]

            def part(i, t, first, last, load=True):
                if not load:
                    return
                g, e = TILES // 2 * i + (FIRST_IN + t // 2), t % 2
                if first == 0:
                    pe.wait_ge(acc_free, TILES * i + (2 * FIRST_IN + t + 1))
                for c in range(first, last):
                    if c % 8 == 0:
                        pe.wait_ge(lo_ready, 4 * g + (2 * e + c // 8 + 1))
                    ins = block_product(e, 2 * e + c // 8, c % 8, h[:, c], c == 0, c == DC - 1)
                    if c % 8 == 7:
                        ins.then_inc(units_done, 1)

            def low_rank(i):
                pe.wait_ge(S("low_ready"), 1)
                pe.wait_ge(S("lora_landed"), 16 * i + 16)
                mm(aux[:, 4, 0:T], lora_w[0:LORA, 0], low[0:LORA, 0], start=True, stop=True)
                mm(aux[:, 4, T:2 * T], lora_w[0:LORA, 1], low[0:LORA, 1], start=True, stop=True) \
                    .then_inc(S("lora_ps"), 1)

            def key_norm(i):
                pe.wait_ge(S("key_squared"), i + 1)
                mm(aux[:, 5, 0:T], mat[:, HEAD_BLOCKS], kn[:], start=True, stop=True).then_inc(S("key_norm_ps"), 1)

            def bonus(i):
                pe.wait_ge(S("bonus_product"), i + 1)
                mm(aux[:, 1, 0:T], mat[:, HEAD_BLOCKS], y_sq[:], start=True, stop=True).then_inc(S("bonus_ps"), 1)

            def turned(i):
                pe.wait_ge(S("keys_ready"), i + 1)
                for k, src in enumerate((rkv[:, 2, 0:P], rkv[:, 2, P:T], kinv[:, 0], binv[:, 0])):
                    ins = nc.tensor.transpose(aux[:, 4, k * P:k * P + P], src, mat[:, IDENT])
                ins.then_inc(S("turned_ps"), 1)

            def grams(j):
                pe.wait_ge(S("queries_ready"), j + 1)
                pe.wait_ge(S("tok_ready"), j + 1)
                pe.wait_ge(S("bonus_ready"), j + 1)
                for c in range(2):
                    for hd, ch in enumerate(heads):
                        ins = mm(aux[:, 4 + hd, c * P:c * P + P], kr[ch, c, 0:P], binv[ch, c], start=True, stop=True)
                ins.then_inc(S("grams_ps"), 1)
                for k, bank in ((binv, 2), (kinv, 0)):
                    if bank == 0:
                        pe.wait_ge(S("qkv_ready"), j + 1)
                    for c in range(2):
                        for hd, ch in enumerate(heads):
                            ins = mm(aux[:, bank + hd, c * 2 * P:(c + 1) * 2 * P], k[ch, c], kr[ch, c], start=True,
                                     stop=True)
                ins.then_inc(S("grams_ps"), 1)

            def w1_level(j, lv):
                pe.wait_ge(S("off_ready"), LEVELS * j + (lv + 1))
                pe.wait_ge(S("inv_t_ready"), (LEVELS + 1) * j + (lv + 1))
                if lv == 0:
                    pe.wait_ge(S("akr_masked"), 2 * j + 2)
                for p in range(4):
                    ins = mm(aux[:, 0, p * P:p * P + P], off[:, p], inv[:, 0, p], start=True, stop=True)
                ins.then_inc(S("w1_ps"), 1)

            def inv_level(j, lv):
                pe.wait_ge(S("w1_ready"), LEVELS * j + (lv + 1))
                pe.wait_ge(S("inv_ready"), LEVELS * j + (lv + 1))
                for p in range(4):
                    ins = mm(aux[:, 2, p * 64:p * 64 + 64], inv[:, 1, p], half_blocks(w1[:, p], lv, 1), start=True,
                             stop=True)
                ins.then_inc(S("inv_t_ps"), 1)
                if lv < LEVELS - 1:
                    for p in range(4):
                        ins = mm(aux[:, 3, p * 64:p * 64 + 64], w1[:, p], half_blocks(inv[:, 1, p], lv, 0),
                                 start=True, stop=True)
                    ins.then_inc(S("inv_ps"), 1)

            def right_side(j, c):
                if c:
                    pe.wait_ge(S("state_ready"), j + 1)
                    mm(aux[:, 0, 0:P], kr[:, 1, 0:P], state[:], start=True, stop=False, skip_group_check=True)
                for hd, v in enumerate(heads):
                    ins = mm(aux[:, 0, v], akr[:, 2 * hd + c, 0:P], tok[:, c, v], start=c == 0, stop=True,
                             skip_group_check=True)
                ins.then_inc(S("ru_ps"), 1)

            def solution(j, c):
                if c == 0:
                    pe.wait_ge(S("inv_t_ready"), (LEVELS + 1) * j + (LEVELS + 1))
                pe.wait_ge(S("ru_ready"), 4 * j + (2 * c + 1))
                for hd, v in enumerate(heads):
                    ins = mm(aux[:, 0, v], inv[:, 0, 2 * hd + c], ru[:, 0, v], start=True, stop=True)
                ins.then_inc(S("ru_ps"), 1)

            def outputs(j, c):
                pe.wait_ge(S("ru_ready"), 4 * j + (2 * c + 2))
                if c == 0:
                    mm(aux[:, 2, 0:P], tok[:, 2], tok[:, 0], start=True, stop=False)
                    mm(aux[:, 2, 0:P], tok[:, 3], ru[:, 1], start=False, stop=True).then_inc(S("state_ps"), 1)
                else:
                    mm(aux[:, 3, P:T], state[:], kr[:, 1, P:2 * P], start=True, stop=False, skip_group_check=True)
                for hd, v in enumerate(heads):
                    dst = aux[v, 3, c * P:c * P + P]
                    mm(dst, tok[:, c, v], akr[:, 2 * hd + c, P:2 * P], start=c == 0, stop=False, skip_group_check=True)
                    ins = mm(dst, ru[:, 1, v], abr[:, 2 * hd + c, P:2 * P], start=False, stop=True,
                             skip_group_check=True)
                if c:
                    ins.then_inc(S("y_ps"), 1)

            def mean_and_gate(j):
                pe.wait_ge(S("y_ready"), j + 1)
                mm(aux[:, 2, 0:T], mat[:, HEAD_BLOCKS], y[:], start=True, stop=True).then_inc(S("mean_ps"), 1)
                pe.wait_ge(S("gate_landed"), 16 * j + 16)
                mm(aux[:, 3, 0:T], gate_w[:, 0], low[:, 2], start=True, stop=False)
                mm(aux[:, 3, 0:T], gate_w[:, 1], low[:, 3], start=False, stop=True).then_inc(S("gate_ps"), 1)

            def square_mean(j):
                pe.wait_ge(S("y_squared"), j + 1)
                mm(aux[:, 0, 0:T], mat[:, HEAD_BLOCKS], y_sq[:], start=True, stop=True).then_inc(S("var_ps"), 1)

            def scores(n):
                pe.wait_ge(S("qkv_ready"), n + 1)
                q, k = qkv[:, 0], qkv[:, 1]
                mm(aux[:, 1, 0:P], q[:, 0:P], k[:, 0:P], start=True, stop=False)
                mm(aux[:, 1, 0:P], ones[:], forget_sel[:, 0:P], start=False, stop=True)
                mm(aux[:, 1, P:3 * P], q[:, P:T], k, start=True, stop=False)
                mm(aux[:, 1, P:3 * P], ones[:], forget_sel[:], start=False, stop=True).then_inc(S("scores_ps"), 1)

            def fox_turned(n):
                pe.wait_ge(S("probs_ready"), n + 1)
                for b in range(3):
                    nc.tensor.transpose(aux[:, 4, b * P:b * P + P], prob[:, b * P:b * P + P], mat[:, IDENT])
                for b in range(2):
                    ins = nc.tensor.transpose(aux[:, 5, b * P:b * P + P], qkv[:, 2, b * P:b * P + P], mat[:, IDENT])
                ins.then_inc(S("fox_turned_ps"), 1)

            def attended(n):
                pe.wait_ge(S("fox_turned"), n + 1)
                mm(aux[:, 1, 0:P], v_tok[:, 0:P], prob_t[:, 0:P], start=True, stop=True)
                mm(aux[:, 1, P:T], v_tok[:, 0:P], prob_t[:, P:2 * P], start=True, stop=False)
                mm(aux[:, 1, P:T], v_tok[:, P:2 * P], prob_t[:, 2 * P:3 * P], start=False, stop=True) \
                    .then_inc(S("attn_ps"), 1)

            def out_blocks(first, last):
                for k in range(first, last):
                    u, b = k // 8, k % 8
                    if b == 0:
                        pe.wait_ge(acc_free, R_OUT + u + 1)
                        pe.wait_ge(lo_ready, 4 * FIRST_OUT + u + 1)
                        pe.wait_ge(S("mixed_ready"), 8)
                    ins = block_product(u % 2, u % SLOTS, b, h[:, b], b == 0, b == 7)
                    if b == 7:
                        ins.then_inc(units_done, 1)

            def body(i, mix, load):
                j, out_too = i - 1, not load
                if mix:
                    grams(j)
                part(i, 0, 0, 16, load)
                part(i, 1, 0, 4, load)
                if out_too:
                    out_blocks(0, 24)
                steps = (
                    (((1, 4, 8),), scores, ((1, 8, 11),)),
                    (((1, 11, 15),), None, ((1, 15, 16), (2, 0, 4))),
                    (((2, 4, 8),), fox_turned, ((2, 8, 11),)),
                    (((2, 11, 15),), attended, ((2, 15, 16), (3, 0, 3))),
                    (((3, 3, 7),), None, ((3, 7, 10),)),
                    (((3, 10, 14),), None, ()))
                for lv, (blocks, attention, more) in enumerate(steps):
                    if mix:
                        w1_level(j, lv)
                    for b in blocks:
                        part(i, *b, load)
                    if out_too:
                        out_blocks(24 + 10 * lv, 28 + 10 * lv)
                    if mix:
                        inv_level(j, lv)
                        if attention is not None:
                            attention(j)
                    if load and lv == 4:
                        low_rank(i)
                    for b in more:
                        part(i, *b, load)
                    if out_too:
                        out_blocks(28 + 10 * lv, 34 + 10 * lv)
                if mix:
                    right_side(j, 0)
                if load:
                    key_norm(i)
                part(i, 3, 14, 16, load)
                part(i, 4, 0, 3, load)
                if out_too:
                    out_blocks(84, 88)
                if mix:
                    solution(j, 0)
                part(i, 4, 3, 7, load)
                if out_too:
                    out_blocks(88, 92)
                if load:
                    bonus(i)
                if mix:
                    outputs(j, 0)
                part(i, 4, 7, 13, load)
                if out_too:
                    out_blocks(92, 98)
                if mix:
                    right_side(j, 1)
                part(i, 4, 13, 16, load)
                if out_too:
                    out_blocks(98, 102)
                if mix:
                    solution(j, 1)
                part(i, 5, 0, 4, load)
                if out_too:
                    out_blocks(102, 106)
                if mix:
                    outputs(j, 1)
                part(i, 5, 4, 8, load)
                if out_too:
                    out_blocks(106, 112)
                if mix:
                    mean_and_gate(j)
                part(i, 5, 8, 11, load)
                if out_too:
                    out_blocks(112, 118)
                if mix:
                    square_mean(j)
                if load:
                    turned(i)
                part(i, 5, 11, 16, load)
                if out_too:
                    out_blocks(118, 128)

            pe.wait_ge(params_landed, 16 * N_PARAMS)
            body(0, False, True)
            with pe.Fori(1, PAIRS) as i:
                body(i, True, True)
            body(PAIRS, True, False)

            with pe.Fori(0, G_OUT // 2) as i:
                for s in range(SLOTS):
                    pe.wait_ge(acc_free, 4 * i + (R_OUT + DC + s + 1))
                    pe.wait_ge(lo_ready, 4 * i + (4 * SECOND_OUT + s + 1))
                    pe.wait_ge(S("mixed_ready"), DC - 1)
                    for b in range(8):
                        if b == 7:
                            pe.wait_ge(S("mixed_ready"), DC)
                        ins = block_product(s % 2, s, b, h[:, 8 + b], b == 0, b == 7)
                    ins.then_inc(units_done, 1)

            for layer in range(2):
                g0, n0, f0 = FIRST_FFN[layer], R_FFN[layer], layer * QUARTERS * G_UP
                for q in range(QUARTERS):
                    def up(i, between=None, each=None):
                        for e in range(2):
                            tile(i + g0, e, e, 2 * i + (n0 + e), h_next, S("h_ready"), DC * (2 * layer + 2),
                                 between if e == 0 else None, each if e == 0 else None)
                    if q == 0:
                        if layer == 0:
                            up(0, between=(1, 0))
                        else:
                            up(0, each=lambda c: add_square(DC + c))
                        with pe.Fori(1, G_UP) as i:
                            up(i)
                    else:
                        with pe.Fori(0, G_UP) as i:
                            up(i)
                    def down_unit(i, s, first, last):
                        if first == 0:
                            pe.wait_ge(acc_free, 4 * i + (n0 + 2 * G_UP + s + 1))
                            pe.wait_ge(lo_ready, 4 * i + (4 * (g0 + G_UP) + s + 1))
                            pe.wait_ge(S("features_ready"), f0 + G_UP - 1)
                        if last == FC:
                            pe.wait_ge(S("features_ready"), f0 + G_UP)
                        for b in range(first, last):
                            ins = block_product(s % 2, s, b, h[:, b], b == 0, b == FC - 1)
                        if last == FC:
                            ins.then_inc(units_done, 1)

                    for first, last in ((0, FC - 1), (FC - 1, FC)):
                        for s in range(2):
                            down_unit(0, s, first, last)
                    for s in range(2, SLOTS):
                        down_unit(0, s, 0, FC)
                    with pe.Fori(1, G_DOWN) as i:
                        for s in range(SLOTS):
                            down_unit(i, s, 0, FC)
                    g0, n0, f0 = g0 + G_QUARTER, n0 + R_QUARTER, f0 + G_UP
                if layer == 1:
                    square_sum(4, 2)
                else:
                    for u, out_chunk in enumerate(POOL_CHUNKS):
                        s, first = u % SLOTS, out_chunk // 4 * 4
                        pe.wait_ge(lo_ready, 4 * FIRST_POOL + u + 1)
                        pe.wait_ge(S("h_ready"), 2 * DC + first + 4)
                        for r in range(2):
                            pe.wait_ge(acc_free, R_POOL + 2 * u + r + (1 if u == 0 else -1))
                            for b in range(4):
                                ins = block_product(2 * (u % 2) + r, s, 4 * r + b, h_next[:, first + b], b == 0, b == 3)
                        ins.then_inc(units_done, 1)
                        if u == 0:
                            square_sum(2, 1)


N_CONSTS, N_PARAMS = 7, 6


POOL_CHUNKS = (8, 10, 12, 14, 0, 2, 4, 6)


def windows(eng, own, c, g, win, pooled, invc):
    tt = eng.tensor_tensor
    src = pooled[:, c]
    for k in range(g + 1):
        dst = win[:, k % 2]
        own.link(tt(dst[:, 16:], src[:, 16:16 + T], src[:, 16 - 2 ** k:16 - 2 ** k + T], ALU.add))
        src = dst
    own.link(tt(src[:, 16:], src[:, 16:], invc[:, g], ALU.mult))
    own.link(tt(pooled[:, c, 16:], src[:, 16:], pooled[:, c, 16:], ALU.subtract))


def _tables():
    import numpy as np
    row, col = np.arange(P)[:, None], np.arange(P)[None, :]
    low = lambda b: (row // (2 * b) == col // (2 * b)) & (row // b % 2 == 1) & (col // b % 2 == 0)
    mats = [low(2 ** (lv + 1)) for lv in range(LEVELS)] + [low(1), low(1).T, row == col, row // 64 == col // 64]
    mats += [np.where(row >= col, 0, -1e30), row < col, row <= col, row > col]
    mats = np.stack([m.astype(np.float32) for m in mats], 1)
    t = np.arange(T)
    count = np.stack([(1 / np.minimum(t + 1, w)).astype(np.float32) for w in (2, 4, 8, 16)])
    return mats, np.broadcast_to(count, (P, 4, T)).copy()


def _layouts(a):
    import numpy as np
    f = {k: np.asarray(v) for k, v in a.items()}
    cols = lambda v: np.ascontiguousarray(v.reshape(-1, P).T)

    def halves(w):
        m = w.shape[1] // P
        return w.reshape(2, 8, P, m, P).transpose(3, 0, 2, 1, 4).reshape(2 * m, P, UA)

    def pad(v, n=P):
        return np.concatenate([v, np.zeros(v.shape[:-1] + (n - v.shape[-1],), v.dtype)], -1)

    W = HEADS * P
    fox, rw = 3 * W + HEADS, 3 * W
    w_in, mu = f["w_in"][0], f["shift_mu"][0]
    wd, ad, gd = fox + rw, fox + rw + LORA, fox + rw + 2 * LORA
    order = [pad(np.concatenate([w_in[:, ad:ad + LORA], w_in[:, 3 * W:fox]], 1)), pad(w_in[:, wd:wd + LORA]),
             w_in[:, gd:]]
    for j in range(PAIRS):
        order += [w_in[:, first + k * W + j * P:first + k * W + j * P + P] for first in (fox, 0) for k in range(3)]
    w_out = np.concatenate([f["w_out"][0][W:], f["w_out"][0][:W]], 0)
    pool = f["w_pool"][0].reshape(4, 4, P, 2, 2, P).transpose(0, 3, 2, 4, 1, 5).reshape(8, P, UA)
    pool = np.concatenate([pool[c // 2:c // 2 + 1] for c in POOL_CHUNKS], 0)
    ups = [halves(w.reshape(D, 2, D_FF // P, P).transpose(0, 2, 1, 3).reshape(D, 2 * D_FF)) for w in f["w_ffn_up"]]
    outs = halves(w_out.reshape(DC, P, D)[list(MIX_ORDER)].reshape(D, D))
    wa = np.concatenate([halves(np.concatenate(order, 1)), outs[0::2], outs[1::2], ups[0], pool, ups[1]], 0)
    wb = np.concatenate([w.reshape(QUARTERS, FC, P, DC, P).transpose(0, 3, 2, 1, 4).reshape(QUARTERS * DC, P, UB)
                         for w in f["w_ffn_down"]], 0)
    mix = np.stack([cols(v) for v in (mu[0:W], mu[W:2 * W], mu[2 * W:3 * W], f["w0"][0], f["a0"][0], f["k_k"][0],
                                      f["k_a"][0], f["r_k"][0].reshape(-1), f["gn_w"][0], f["gn_b"][0])], 2)
    wd, ad, gd = rw, rw + LORA, rw + 2 * LORA
    mu0 = np.stack([pad(mu[ad:ad + LORA]), pad(mu[wd:wd + LORA]), mu[gd:gd + P], mu[gd + P:gd + 2 * P]], 1)
    b_f = np.zeros((P, 1), np.float32)
    b_f[LORA:LORA + HEADS, 0] = f["b_f"][0]
    rows = lambda w: pad(w.T).T.reshape(P, PAIRS, P).transpose(1, 0, 2)
    gate = f["w_gate_up"][0].reshape(2, P, PAIRS, P).transpose(2, 1, 0, 3)
    lora = np.concatenate([rows(f["w_iclr_up"][0])[:, :, None], rows(f["w_decay_up"][0])[:, :, None], gate], 2)
    lora = np.concatenate([lora, np.zeros((1,) + lora.shape[1:], lora.dtype)], 0)
    conv = np.concatenate([f["conv_w"], f["conv_b"][:, None]], 1)
    conv = conv.reshape(2, 4, 2, D_FF // P, P).transpose(4, 0, 3, 2, 1).reshape(P, -1, 4)
    gains = np.stack([cols(v) for v in (f["mix_norm"][0], f["pool_norm"][0], f["ffn_norm"][0], f["ffn_norm"][1],
                                        f["final_norm"])], 1)
    x = f["x"][0].T.reshape(DC, P, T).transpose(1, 0, 2)
    mats, count = _tables()
    named = dict(x_in=x, gains=gains, wa=wa, wb=wb, mix_p=mix, mu0=mu0, b_f=b_f, lora=lora, conv_p=conv,
                 pool_p=cols(f["pool_scale"][0]), mats=mats, inv_count=count)
    return {k: np.ascontiguousarray(v) for k, v in named.items()}


def kernel(**inputs):
    import concourse.bacc as _bacc
    from concourse.bass_utils import run_bass_kernel_spmd as _run

    nc = _bacc.Bacc("TRN2", target_bir_lowering=False, num_devices=1)
    arrays = _layouts(inputs)
    args = {k: nc.dram_tensor(f"{k}_dram", v.shape, mybir.dt.from_np(v.dtype), kind="ExternalInput").ap()
            for k, v in arrays.items()}
    out = nc.dram_tensor("out_dram", (P, DC, T), F32, kind="ExternalOutput").ap()
    trunk(nc, out=out, **args)
    r = _run(nc, [{f"{k}_dram": v for k, v in arrays.items()}], core_ids=[0])
    return r.results[0]["out_dram"].transpose(2, 1, 0).reshape(1, T, D)
```
